# Optimizing a Trainium2 kernel written in Bass

```python
import jax, jax.numpy as jnp
from jax import lax
import numpy as np

D_MODEL = 2048
BATCH = 1
SEQ = 256
DEPTH = 1

N_MIXERS = 3
CHUNK = 128
A_WIDTH = D_MODEL
A_HEADS = 8
A_HEAD_DIM = A_WIDTH // A_HEADS
B_WIDTH = D_MODEL
B_GROUPS = 4
B_GROUP_DIM = B_WIDTH // B_GROUPS
POOL_WINDOWS = (2, 4, 8, 16)
C_WIDTH = D_MODEL
CONV_WIDTH = 31
N_EXPERTS = 16
N_GROUPS = 4
EXPERTS_PER_GROUP = N_EXPERTS // N_GROUPS
TOP_K = 2
D_EXPERT = D_MODEL // 2
EXPERT_BLOCK = 128
RMS_EPS = 1e-6
LN_EPS = 1e-5

kernel_name = 'hybrid_gmlp_pool_conformer_grouped_moe'

def rmsnorm(x, g):
    xf = x.astype(jnp.float32)
    y = xf * lax.rsqrt(jnp.mean(xf * xf, axis=-1, keepdims=True) + RMS_EPS)
    return (y * g.astype(jnp.float32)).astype(x.dtype)

def mixer_gmlp(h, w_in, v_gain, w_s, b_s, w_out):
    bsz, s, _ = h.shape
    z = jax.nn.gelu(h @ w_in)
    u, v = jnp.split(z, 2, axis=-1)
    v = rmsnorm(v, v_gain)
    v5 = v.reshape(bsz, s // CHUNK, CHUNK, A_HEADS, A_HEAD_DIM)
    causal = jnp.tril(jnp.ones((CHUNK, CHUNK), dtype=w_s.dtype))
    sv = jnp.einsum('hts,bcshd->bcthd', w_s * causal, v5) + b_s.T[None, None, :, :, None]
    return (u * sv.reshape(bsz, s, A_WIDTH)) @ w_out

def mixer_pool(h, w_in, w_grp, b_grp, scale, w_out):
    bsz, s, _ = h.shape
    p = h @ w_in
    c = jnp.cumsum(p.astype(jnp.float32), axis=1).reshape(bsz, s, B_GROUPS, B_GROUP_DIM)
    prev = jnp.stack(
        [jnp.pad(c[:, : s - w, g], ((0, 0), (w, 0), (0, 0))) for g, w in enumerate(POOL_WINDOWS)],
        axis=2)
    pos = jnp.arange(s, dtype=jnp.int32)
    win = jnp.array(POOL_WINDOWS, dtype=jnp.int32)
    count = jnp.minimum(pos[:, None] + 1, win[None, :]).astype(jnp.float32)
    pooled = (c - prev) / count[None, :, :, None]
    mix = pooled.astype(p.dtype) - p.reshape(bsz, s, B_GROUPS, B_GROUP_DIM)
    z = jnp.einsum('bsgc,gcd->bsgd', mix, w_grp) + b_grp[None, None]
    z = z.reshape(bsz, s, B_WIDTH) * scale
    return z @ w_out

def mixer_conv(h, w_in, dw_w, dw_b, ln_g, ln_b, w_out):
    z = h @ w_in
    a, gate = jnp.split(z, 2, axis=-1)
    g = a * jax.nn.sigmoid(gate)
    y = lax.conv_general_dilated(
        g, dw_w[:, None, :].astype(g.dtype), window_strides=(1,),
        padding=[(CONV_WIDTH - 1, 0)], dimension_numbers=('NWC', 'WIO', 'NWC'),
        feature_group_count=C_WIDTH) + dw_b
    yf = y.astype(jnp.float32)
    mu = jnp.mean(yf, axis=-1, keepdims=True)
    var = jnp.mean(jnp.square(yf - mu), axis=-1, keepdims=True)
    yn = ((yf - mu) * lax.rsqrt(var + LN_EPS) * ln_g.astype(jnp.float32)
          + ln_b.astype(jnp.float32)).astype(g.dtype)
    return jax.nn.silu(yn) @ w_out

def grouped_moe(y, router_w, router_b, w_gate, w_up, w_down):
    bsz, s, d = y.shape
    n = bsz * s
    xf = y.reshape(n, d)
    probs = jax.nn.softmax((xf @ router_w).astype(jnp.float32), axis=-1)
    sel = (probs + router_b.astype(jnp.float32)).reshape(n, N_GROUPS, EXPERTS_PER_GROUP)
    group_score = jnp.sum(lax.top_k(sel, TOP_K)[0], axis=-1)
    grp = jnp.argmax(group_score, axis=-1).astype(jnp.int32)
    in_group = jnp.take_along_axis(sel, grp[:, None, None], axis=1)[:, 0]
    _, loc = lax.top_k(in_group, TOP_K)
    idx = grp[:, None] * EXPERTS_PER_GROUP + loc.astype(jnp.int32)
    gw = jnp.take_along_axis(probs, idx, axis=-1)
    gw = gw / jnp.sum(gw, axis=-1, keepdims=True)

    n_assign = n * TOP_K
    flat_e = idx.reshape(n_assign)
    flat_tok = jnp.repeat(jnp.arange(n, dtype=jnp.int32), TOP_K)
    flat_w = gw.reshape(n_assign)
    order = jnp.argsort(flat_e)
    se, stok, sw = flat_e[order], flat_tok[order], flat_w[order]
    counts = jnp.bincount(flat_e, length=N_EXPERTS).astype(jnp.int32)
    pcounts = (counts + EXPERT_BLOCK - 1) // EXPERT_BLOCK * EXPERT_BLOCK
    starts = jnp.cumsum(counts) - counts
    pends = jnp.cumsum(pcounts)
    pstarts = pends - pcounts
    dest = pstarts[se] + jnp.arange(n_assign, dtype=jnp.int32) - starts[se]
    n_rows = n_assign + N_EXPERTS * EXPERT_BLOCK
    n_blocks = n_rows // EXPERT_BLOCK
    tok_buf = jnp.full((n_rows,), n, dtype=jnp.int32).at[dest].set(stok)
    w_buf = jnp.zeros((n_rows,), dtype=jnp.float32).at[dest].set(sw)
    block_e = jnp.minimum(
        jnp.searchsorted(pends, jnp.arange(n_blocks, dtype=jnp.int32) * EXPERT_BLOCK, side='right'),
        N_EXPERTS - 1).astype(jnp.int32)
    x_pad = jnp.concatenate([xf, jnp.zeros((1, d), xf.dtype)], axis=0)
    xb = x_pad[tok_buf].reshape(n_blocks, EXPERT_BLOCK, d)

    def expert_block(args):
        xblk, e = args
        hid = jax.nn.silu(xblk @ w_gate[e]) * (xblk @ w_up[e])
        return hid @ w_down[e]

    yb = lax.map(expert_block, (xb, block_e)).reshape(n_rows, d)
    out = jax.ops.segment_sum(yb * w_buf[:, None].astype(yb.dtype), tok_buf, num_segments=n + 1)[:n]
    return out.reshape(bsz, s, d)

def setup_inputs(seed: int = 0) -> dict:
    key = jax.random.key(seed)
    ks = iter(jax.random.split(key, 32))
    nrm = lambda shape, scale: jax.random.normal(next(ks), shape, jnp.float32) * scale
    na, nb, nc = (len(range(m, DEPTH, N_MIXERS)) for m in range(N_MIXERS))
    out_scale = (2.0 * DEPTH) ** -0.5
    return {
        'x': nrm((BATCH, SEQ, D_MODEL), 1.0),
        'norm_mix_g': 1.0 + nrm((DEPTH, D_MODEL), 0.05),
        'norm_ffn_g': 1.0 + nrm((DEPTH, D_MODEL), 0.05),
        'final_g': 1.0 + nrm((D_MODEL,), 0.05),
        'a_w_in': nrm((na, D_MODEL, 2 * A_WIDTH), D_MODEL ** -0.5),
        'a_v_gain': 1.0 + nrm((na, A_WIDTH), 0.05),
        'a_w_s': nrm((na, A_HEADS, CHUNK, CHUNK), 0.5 * CHUNK ** -0.5),
        'a_b_s': 1.0 + nrm((na, A_HEADS, CHUNK), 0.1),
        'a_w_out': nrm((na, A_WIDTH, D_MODEL), A_WIDTH ** -0.5 * out_scale),
        'b_w_in': nrm((nb, D_MODEL, B_WIDTH), D_MODEL ** -0.5),
        'b_w_grp': nrm((nb, B_GROUPS, B_GROUP_DIM, B_GROUP_DIM), B_GROUP_DIM ** -0.5),
        'b_b_grp': nrm((nb, B_GROUPS, B_GROUP_DIM), 0.02),
        'b_scale': 1.0 + nrm((nb, B_WIDTH), 0.1),
        'b_w_out': nrm((nb, B_WIDTH, D_MODEL), B_WIDTH ** -0.5 * out_scale),
        'c_w_in': nrm((nc, D_MODEL, 2 * C_WIDTH), D_MODEL ** -0.5),
        'c_dw_w': nrm((nc, CONV_WIDTH, C_WIDTH), CONV_WIDTH ** -0.5),
        'c_dw_b': nrm((nc, C_WIDTH), 0.02),
        'c_ln_g': 1.0 + nrm((nc, C_WIDTH), 0.05),
        'c_ln_b': nrm((nc, C_WIDTH), 0.02),
        'c_w_out': nrm((nc, C_WIDTH, D_MODEL), C_WIDTH ** -0.5 * out_scale),
        'router_w': nrm((D_MODEL, N_EXPERTS), D_MODEL ** -0.5),
        'router_b': nrm((N_EXPERTS,), 0.01),
        'moe_w_gate': nrm((DEPTH, N_EXPERTS, D_MODEL, D_EXPERT), D_MODEL ** -0.5),
        'moe_w_up': nrm((DEPTH, N_EXPERTS, D_MODEL, D_EXPERT), D_MODEL ** -0.5),
        'moe_w_down': nrm((DEPTH, N_EXPERTS, D_EXPERT, D_MODEL), D_EXPERT ** -0.5 * out_scale),
    }

def reference(x, norm_mix_g, norm_ffn_g, final_g,
              a_w_in, a_v_gain, a_w_s, a_b_s, a_w_out,
              b_w_in, b_w_grp, b_b_grp, b_scale, b_w_out,
              c_w_in, c_dw_w, c_dw_b, c_ln_g, c_ln_b, c_w_out,
              router_w, router_b, moe_w_gate, moe_w_up, moe_w_down):
    h = x
    for i in range(DEPTH):
        m, j = i % N_MIXERS, i // N_MIXERS
        y = rmsnorm(h, norm_mix_g[i])
        if m == 0:
            mix = mixer_gmlp(y, a_w_in[j], a_v_gain[j], a_w_s[j], a_b_s[j], a_w_out[j])
        elif m == 1:
            mix = mixer_pool(y, b_w_in[j], b_w_grp[j], b_b_grp[j], b_scale[j], b_w_out[j])
        else:
            mix = mixer_conv(y, c_w_in[j], c_dw_w[j], c_dw_b[j], c_ln_g[j], c_ln_b[j], c_w_out[j])
        h = h + mix
        y = rmsnorm(h, norm_ffn_g[i])
        h = h + grouped_moe(y, router_w, router_b, moe_w_gate[i], moe_w_up[i], moe_w_down[i])
    return rmsnorm(h, final_g)


_drawn_inputs = setup_inputs


def setup_inputs(seed=0):
    import zlib

    import numpy as np

    out = dict(_drawn_inputs(seed))
    spreads = {}
    factors = {}
    for name, (base, spread) in spreads.items():
        noise = np.random.default_rng([zlib.crc32(name.encode()), seed]).standard_normal(out[name].shape)
        drawn = base * np.exp(spread * noise) if base else spread * noise
        out[name] = __import__('jax').numpy.asarray(drawn.astype(out[name].dtype))
    for name, factor in factors.items():
        out[name] = (out[name] * factor).astype(out[name].dtype)
    return out
```

```python
import concourse.bass as bass
from concourse import mybir
from contextlib import ExitStack


def hybrid_trunk_kernel(nc, x_in, norm_mix_g, norm_ffn_g, final_g, a_w_in, a_v_gain, a_w_s, a_b_s,
                        a_w_out, router_w, router_b, w_gate, w_up, w_down, out):
    f32, f32r, i32 = mybir.dt.float32, mybir.dt.float32r, mybir.dt.int32
    ALU = mybir.AluOpType
    ACT = mybir.ActivationFunctionType
    AX = mybir.AxisListType

    P = 128
    SEQ, D = x_in.shape[1], x_in.shape[2]
    NB = SEQ // P
    KD = D // P
    HEADS, CHUNK = a_w_s.shape[1], a_w_s.shape[2]
    HD = D // HEADS
    E, F = w_gate.shape[1], w_gate.shape[3]
    GROUPS = 4
    PER_GROUP = E // GROUPS
    TOK = 64
    BANK = 512
    PIECE = 1024
    RING = 12
    PIECE_UNITS = KD // 2
    PIECES_IN, PIECES_OUT = 2 * D // PIECE, D // PIECE
    PIECES = PIECES_IN + PIECES_OUT
    ITEM_UNITS = 24
    STEPS = 16
    KF = F // P
    MORE = 8
    MAX_ITEMS = E + MORE
    RMS_EPS = 1e-6
    BIG = 1e30
    FAR = 1000.0

    with ExitStack() as ctx:
        def sb(name, shape, dt=f32, at=ctx):
            return at.enter_context(nc.sbuf_tensor(name, shape, dt))

        def sem(name):
            return ctx.enter_context(nc.semaphore(name))

        ring = sb("ring", [P, RING, 2048])
        x = sb("x", [P, NB, D])
        gain_bc = sb("gain_bc", [P, D])
        ident = sb("ident", [P, P])
        vec_cols = sb("vec_cols", [P, 2 * KD + HEADS])
        rw = sb("rw", [P, KD, E])
        rb = sb("rb", [P, 1, E])
        eps = sb("eps", [P, 1])
        ss = sb("ss", [P, 8])
        root = sb("root", [P, 8])
        rinv = sb("rinv", [P, 8])

        mix = ExitStack()
        z = sb("z", [P, 2, NB, D], at=mix)
        ws_t = sb("ws_t", [P, HEADS, CHUNK], at=mix)
        act_hi = sb("act_hi", [P, KD, SEQ], f32r, at=mix)
        act_lo = sb("act_lo", [P, KD, SEQ], f32r, at=mix)
        w_hi = sb("w_hi", [P, 2, PIECE], f32r, at=mix)
        w_lo = sb("w_lo", [P, 2, PIECE], f32r, at=mix)
        v, u = z[:, 0, :, :], z[:, 1, :, :]
        scratch = z[:, 1, :, :].rearrange("p n d -> p (n d)")
        ws_raw = scratch[:, 0:HEADS * CHUNK].rearrange("p (h s) -> p h s", h=HEADS)
        xg_t = scratch[:, 1024:2048].rearrange("p (b k n) -> p b k n", b=2, k=2)
        vec_raw = scratch[0:2 * KD + HEADS, 2048:2176]
        mix.close()

        h2_t = sb("h2_t", [P, KD, SEQ])
        acc = sb("acc", [P, NB, D])
        before = sb("before", [P, P])
        ones = sb("ones", [P, P])
        tok_of = sb("tok_of", [P, 2 * TOK])
        tok_i = sb("tok_i", [P, 2 * TOK], i32)
        e_idx = sb("e_idx", [P, 1, E])
        e_i = sb("e_i", [P, E], i32)
        rev = sb("rev", [P, 1, E])
        rev_i = sb("rev_i", [P, E], i32)
        q_idx = sb("q_idx", [P, MORE, 1])
        q_i = sb("q_i", [P, MORE], i32)
        xg = sb("xg", [P, KD, TOK])
        sil = sb("sil", [P, BANK])
        hid = sb("hid", [P, BANK])
        hid_t = sb("hid_t", [P, 4, 2 * TOK])
        y = sb("y", [P, 2, BANK])
        back = sb("back", [P, SEQ])
        pick = sb("pick", [P, NB, TOK])
        place = sb("place", [P, NB, 2 * TOK])
        rwg = sb("rwg", [P, KD, E])
        logit = sb("logit", [P, NB, E])
        shifted = sb("shifted", [P, NB, E])
        expd = sb("expd", [P, NB, E])
        probs = sb("probs", [P, NB, E])
        sel = sb("sel", [P, NB, E])
        red = sb("red", [P, NB, 12])
        pairs = sb("pairs", [P, NB, GROUPS, 6])
        gscore = sb("gscore", [P, NB, GROUPS, 1])
        gkey = sb("gkey", [P, NB, GROUPS, 1])
        gpick = sb("gpick", [P, NB, GROUPS, 1])
        gpen = sb("gpen", [P, NB, GROUPS, 1])
        masked = sb("masked", [P, NB, E])
        key = sb("key", [P, NB, E])
        first = sb("first", [P, NB, E])
        assigned = sb("assigned", [P, NB, E])
        wsel = sb("wsel", [P, NB, E])
        rank_t = sb("rank_t", [P, NB, E])
        extra = sb("extra", [P, 1, E])
        upto = sb("upto", [P, 1, E])
        start = sb("start", [P, 1, E])
        qa = sb("qa", [P, MORE, E])
        qsel = sb("qsel", [P, MORE, E])
        qoff = sb("qoff", [P, MORE, E])
        qt = sb("qt", [P, MORE, E])
        rank_of = sb("rank_of", [P, NB, MAX_ITEMS + 2])
        weight_of = sb("weight_of", [P, NB, MAX_ITEMS + 2])
        ids_f = sb("ids_f", [P, MAX_ITEMS])
        item_expert = sb("item_expert", [P, MAX_ITEMS], i32)
        count_f = sb("count_f", [P, 1])
        item_count = sb("item_count", [P, 1], i32)

        bank = [ctx.enter_context(nc.psum_tensor(f"bank{b}", [P, BANK], f32)) for b in range(8)]

        x_loaded = [sem(f"x_loaded{b}") for b in range(NB)]
        vecs_loaded = sem("vecs_loaded")
        ws_loaded = sem("ws_loaded")
        router_loaded = sem("router_loaded")
        gain_loaded = sem("gain_loaded")
        unit_loaded = [sem(f"unit_loaded{s}") for s in range(RING)]
        ident_ready = sem("ident_ready")
        ws_masked = sem("ws_masked")
        vecs_transposed = sem("vecs_transposed")
        vecs_ready = sem("vecs_ready")
        x_transposed = sem("x_transposed")
        x_scaled = sem("x_scaled")
        act_hi_ready = sem("act_hi_ready")
        act_ready = sem("act_ready")
        ws_transposed = sem("ws_transposed")
        ws_ready = sem("ws_ready")
        hi_split = sem("hi_split")
        tile_split = sem("tile_split")
        tile_used = sem("tile_used")
        sq_done = sem("sq_done")
        roots_done = sem("roots_done")
        rinv_ready = sem("rinv_ready")
        z_ready = sem("z_ready")
        v_ready = sem("v_ready")
        mixed = sem("mixed")
        gated = sem("gated")
        gated_t = sem("gated_t")
        h2_ready = sem("h2_ready")
        h2_transposed = sem("h2_transposed")
        h2_t_ready = sem("h2_t_ready")
        consts_ready = sem("consts_ready")
        pool_step = sem("pool_step")
        rwg_ready = sem("rwg_ready")
        logits_done = sem("logits_done")
        shifted_ready = sem("shifted_ready")
        exp_done = sem("exp_done")
        assigned_ready = sem("assigned_ready")
        ranks_done = sem("ranks_done")
        tables_ready = sem("tables_ready")
        chain = sem("chain")
        acc_set = sem("acc_set")
        pick_ready = sem("pick_ready")
        gathered = sem("gathered")
        xg_ready = sem("xg_ready")
        step_done = sem("step_done")
        sil_ready = sem("sil_ready")
        hid_ready = sem("hid_ready")
        hid_transposed = sem("hid_transposed")
        hid_t_ready = sem("hid_t_ready")
        y_ready = sem("y_ready")
        place_transposed = sem("place_transposed")
        back_ready = sem("back_ready")
        scattered = sem("scattered")
        acc_added = sem("acc_added")
        out_ready = sem("out_ready")
        stored = sem("stored")

        w_in_v = a_w_in[0].rearrange("(k p) c -> p k c", p=P)
        w_out_v = a_w_out[0].rearrange("(k p) c -> p k c", p=P)
        gate_v = w_gate[0].rearrange("e (k p) c -> p e k c", p=P)
        up_v = w_up[0].rearrange("e (k p) c -> p e k c", p=P)
        down_v = w_down[0].rearrange("e (k p) c -> p e k c", p=P)
        x_v = x_in[0].rearrange("(b p) d -> p b d", p=P)
        out_v = out[0].rearrange("(b p) d -> p b d", p=P)

        def slot_of(unit):
            return (unit + PIECE_UNITS) % RING

        def loads_before(unit):
            slot = slot_of(unit)
            return (PIECES if slot < PIECE_UNITS else 0) + (1 if unit < RING else 2)

        def step_of(unit):
            return unit // 2 if unit < 2 * PIECE_UNITS else unit - PIECE_UNITS

        block = ctx.enter_context(nc.Block())

        @block.sync
        def _(sp):
            for b in range(NB):
                sp.dma_start(x[:, b, :], x_v[:, b, :]).then_inc(x_loaded[b], 16)

            for p in range(PIECES):
                for j in range(PIECE_UNITS):
                    if p >= 1:
                        sp.wait_ge(tile_split, KD * (p - 1) + 2 * j + 2)
                    if p < PIECES_IN:
                        c = ((p + 2) % PIECES_IN) * PIECE
                        src = w_in_v[:, 2 * j:2 * j + 2, c:c + PIECE]
                    else:
                        c = (p - PIECES_IN) * PIECE
                        src = w_out_v[:, 2 * j:2 * j + 2, c:c + PIECE]
                    sp.dma_start(ring[:, j, :].rearrange("p (k c) -> p k c", k=2), src)\
                      .then_inc(unit_loaded[j], 16)
                if p == PIECES_IN:
                    sp.wait_ge(v_ready, NB)
                    sp.dma_start(gain_bc[:, :], final_g.rearrange("(a d) -> a d", a=1).to_broadcast([P, D]))\
                      .then_inc(gain_loaded, 16)

            def load_unit(expert, unit):
                slot = slot_of(unit)
                if unit < 2 * PIECE_UNITS:
                    m, w = unit // 2, (gate_v, up_v)[unit % 2]
                    src = w[:, expert, 2 * m:2 * m + 2, :]
                    dst = ring[:, slot, :].rearrange("p (k c) -> p k c", k=2)
                    if not isinstance(expert, int):
                        dst = dst.unsqueeze(1)
                else:
                    src = down_v[:, expert, unit - 2 * PIECE_UNITS, :]
                    dst = ring[:, slot, :]
                    if not isinstance(expert, int):
                        dst = dst.unsqueeze(1)
                sp.dma_start(dst, src).then_inc(unit_loaded[slot], 16)

            for unit in range(ITEM_UNITS):
                if RING - PIECE_UNITS <= unit < RING:
                    sp.wait_ge(tile_split, KD * (PIECES - 1) + 2 * slot_of(unit) + 2)
                elif unit >= RING:
                    sp.wait_ge(step_done, step_of(unit - RING) + 1)
                load_unit(0, unit)

            sp.wait_ge(tables_ready, 1)
            n_items = sp.value_load(item_count[0:1, 0:1], min_val=E, max_val=MAX_ITEMS)
            with sp.Fori(1, n_items) as i:
                expert = bass.ds(sp.value_load(item_expert[0:1, bass.ds(i, 1)], min_val=0, max_val=E - 1), 1)
                for unit in range(ITEM_UNITS):
                    if unit < RING:
                        sp.wait_ge(step_done, i * STEPS + (step_of(unit + RING) + 1 - STEPS))
                    else:
                        sp.wait_ge(step_done, i * STEPS + (step_of(unit - RING) + 1))
                    load_unit(expert, unit)

            for n in range(2 * NB):
                b, c = n // 2, n % 2 * PIECE
                sp.wait_ge(out_ready, n + 1)
                sp.dma_start(out_v[:, b, c:c + PIECE], acc[:, b, c:c + PIECE]).then_inc(stored, 16)
            sp.wait_ge(stored, 16 * 2 * NB)

        @block.gpsimd
        def _(pool):
            nc.gpsimd.memset(ident[:, :], 0.0).then_inc(pool_step, 1)
            nc.gpsimd.memset(eps[:, :], RMS_EPS).then_inc(pool_step, 1)
            pool.wait_ge(pool_step, 2)
            nc.gpsimd.affine_select(out=ident[:, :], in_=ident[:, :], compare_op=ALU.not_equal, fill=1.0,
                                    base=0, pattern=[[-1, P]], channel_multiplier=1).then_inc(ident_ready, 1)
            pool.wait_ge(ws_loaded, 16)
            nc.gpsimd.affine_select(out=ws_raw, in_=ws_raw, compare_op=ALU.is_ge, fill=0.0, base=0,
                                    pattern=[[0, HEADS], [-1, CHUNK]], channel_multiplier=1).then_inc(ws_masked, 1)
            pool.wait_ge(mixed, HEADS)
            nc.gpsimd.memset(ones[:, :], 1.0).then_inc(pool_step, 1)
            nc.gpsimd.memset(before[:, :], 1.0).then_inc(pool_step, 1)
            nc.gpsimd.iota(tok_i[:, :], pattern=[[0, 2], [1, TOK]], base=0, channel_multiplier=0).then_inc(pool_step, 1)
            nc.gpsimd.iota(e_i[:, :], pattern=[[1, E]], base=0, channel_multiplier=0).then_inc(pool_step, 1)
            nc.gpsimd.iota(rev_i[:, :], pattern=[[-1, E]], base=E, channel_multiplier=0).then_inc(pool_step, 1)
            nc.gpsimd.iota(q_i[:, :], pattern=[[1, MORE]], base=0, channel_multiplier=0).then_inc(pool_step, 1)
            pool.wait_ge(pool_step, 8)
            nc.gpsimd.affine_select(out=before[:, :], in_=before[:, :], compare_op=ALU.is_gt, fill=0.0, base=0,
                                    pattern=[[1, P]], channel_multiplier=-1).then_inc(consts_ready, 1)
            nc.gpsimd.tensor_copy(tok_of[:, :], tok_i[:, :]).then_inc(consts_ready, 1)
            nc.gpsimd.tensor_copy(e_idx[:, 0, :], e_i[:, :]).then_inc(consts_ready, 1)
            nc.gpsimd.tensor_copy(rev[:, 0, :], rev_i[:, :]).then_inc(consts_ready, 1)
            nc.gpsimd.tensor_copy(q_idx[:, :, 0], q_i[:, :]).then_inc(consts_ready, 1)
            pool.wait_ge(tile_used, KD * PIECES)
            nc.gpsimd.memset(rank_of[:, :, :], -FAR).then_inc(consts_ready, 1)
            nc.gpsimd.memset(weight_of[:, :, :], 0.0).then_inc(consts_ready, 1)
            nc.gpsimd.memset(y[:, :, :], 0.0).then_inc(y_ready, 1)
            nc.gpsimd.memset(back[:, :], 0.0).then_inc(back_ready, 1)

        @block.scalar
        def _(act):
            act.dma_start(vec_raw[0:KD, :], norm_mix_g[0].rearrange("(k p) -> k p", p=P)).then_inc(vecs_loaded, 16)
            act.dma_start(vec_raw[KD:2 * KD, :], norm_ffn_g[0].rearrange("(k p) -> k p", p=P)).then_inc(vecs_loaded, 16)
            act.dma_start(vec_raw[2 * KD:2 * KD + HEADS, :], a_b_s[0]).then_inc(vecs_loaded, 16)
            act.dma_start(ws_raw, a_w_s[0].rearrange("h t s -> t h s")).then_inc(ws_loaded, 16)
            act.dma_start(gain_bc[:, :], a_v_gain.to_broadcast([P, D])).then_inc(gain_loaded, 16)
            act.dma_start(rw[:, :, :], router_w.rearrange("(k p) e -> p k e", p=P)).then_inc(router_loaded, 16)
            act.dma_start(rb[:, 0, :], router_b.rearrange("(a e) -> a e", a=1).to_broadcast([P, E]))\
               .then_inc(router_loaded, 16)

            act.wait_ge(vecs_transposed, 1)
            nc.scalar.copy(vec_cols[:, :], bank[0][:, 0:2 * KD + HEADS]).then_inc(vecs_ready, 1)
            for g in range(KD // 2):
                act.wait_ge(x_scaled, g + 1)
                nc.scalar.copy(act_hi[:, 2 * g:2 * g + 2, :], xg_t[:, g % 2, :, :]).then_inc(act_hi_ready, 1)
            for g in range(2):
                act.wait_ge(ws_transposed, g + 1)
                nc.scalar.copy(ws_t[:, 4 * g:4 * g + 4, :].rearrange("p h s -> p (h s)"), bank[4 + g][:, :])\
                  .then_inc(ws_ready, 1)
            for b in range(NB):
                act.wait_ge(x_loaded[b], 16)
                nc.scalar.activation(v[:, b, :], x[:, b, :], ACT.Square, accum_out=ss[:, b:b + 1]).then_inc(sq_done, 1)
            act.wait_ge(sq_done, NB)
            nc.scalar.activation(root[:, 0:2], ss[:, 0:2], ACT.Sqrt, bias=eps[:, 0:1], scale=1.0 / D)\
              .then_inc(roots_done, 1)

            def gelu_piece(p):
                half, c0 = p // 2, p % 2 * PIECE
                act.wait_ge(tile_used, KD * (p + 1))
                for c in range(2):
                    for b in range(NB):
                        last = nc.scalar.activation(z[:, half, b, c0 + c * BANK:c0 + (c + 1) * BANK],
                                                    bank[4 * (p % 2) + 2 * c + b][:, :], ACT.Gelu_apprx_tanh,
                                                    scale=rinv[:, b:b + 1])
                        last.then_inc(z_ready, 1)

            act.wait_ge(rinv_ready, 1)
            gelu_piece(0)
            gelu_piece(1)
            act.wait_ge(z_ready, 8)
            for b in range(NB):
                nc.scalar.activation(u[:, b, :], v[:, b, :], ACT.Square, accum_out=ss[:, 2 + b:3 + b])\
                  .then_inc(sq_done, 1)
            act.wait_ge(sq_done, 2 * NB)
            nc.scalar.activation(root[:, 2:4], ss[:, 2:4], ACT.Sqrt, bias=eps[:, 0:1], scale=1.0 / D)\
              .then_inc(roots_done, 1)
            gelu_piece(2)
            gelu_piece(3)
            for h in range(HEADS):
                act.wait_ge(gated_t, h + 1)
                nc.scalar.copy(act_hi[:, 2 * h:2 * h + 2, :].rearrange("p k n -> p (k n)"), bank[h][:, :])\
                  .then_inc(act_hi_ready, 1)
            for half in range(2):
                act.wait_ge(h2_ready, 4 * (half + 1))
                for b in range(NB):
                    nc.scalar.activation(acc[:, b, half * PIECE:(half + 1) * PIECE],
                                         x[:, b, half * PIECE:(half + 1) * PIECE], ACT.Square,
                                         accum_out=root[:, 2 * half + b:2 * half + b + 1]).then_inc(sq_done, 1)
                for g in range(4):
                    act.wait_ge(h2_transposed, 4 * half + g + 1)
                    nc.scalar.copy(h2_t[:, 8 * half + 2 * g:8 * half + 2 * g + 2, :].rearrange("p k n -> p (k n)"),
                                   bank[g][:, :]).then_inc(h2_t_ready, 1)
            act.wait_ge(rinv_ready, 3)
            nc.scalar.activation(root[:, 4:6], ss[:, 4:6], ACT.Sqrt, bias=eps[:, 0:1], scale=1.0 / D)\
              .then_inc(roots_done, 1)
            act.wait_ge(shifted_ready, 1)
            nc.scalar.activation(expd[:, :, :], shifted[:, :, :], ACT.Exp).then_inc(exp_done, 1)
            act.wait_ge(sq_done, 4 * NB)
            for b in range(NB):
                nc.scalar.copy(acc[:, b, :], x[:, b, :]).then_inc(acc_set, 1)

            act.wait_ge(tables_ready, 1)
            n_items = act.value_load(item_count[0:1, 0:1], min_val=E, max_val=MAX_ITEMS)
            with act.Fori(0, n_items) as i:
                act.wait_ge(step_done, i * STEPS + STEPS // 2)
                nc.scalar.activation(sil[TOK:P, :], bank[0][0:TOK, :], ACT.Silu).then_inc(sil_ready, 1)
                nc.scalar.activation(sil[0:TOK, :], bank[1][TOK:P, :], ACT.Silu).then_inc(sil_ready, 1)
                act.wait_ge(place_transposed, i + 1)
                nc.scalar.copy(back[:, :], bank[5][:, 0:SEQ]).then_inc(back_ready, 1)
                act.wait_ge(hid_transposed, i + 1)
                nc.scalar.copy(hid_t[:, :, :].rearrange("p f t -> p (f t)"), bank[4][:, :]).then_inc(hid_t_ready, 1)
                act.wait_ge(step_done, i * STEPS + STEPS)
                nc.scalar.copy(y[:, 0, :], bank[2][:, :])
                nc.scalar.copy(y[:, 1, :], bank[3][:, :]).then_inc(y_ready, 1)

            act.wait_ge(acc_added, (n_items + 1) * 8)
            for b in range(NB):
                nc.scalar.activation(x[:, b, :], acc[:, b, :], ACT.Square, accum_out=ss[:, 6 + b:7 + b])\
                  .then_inc(sq_done, 1)
            act.wait_ge(sq_done, 5 * NB)
            nc.scalar.activation(root[:, 6:8], ss[:, 6:8], ACT.Sqrt, bias=eps[:, 0:1], scale=1.0 / D)\
              .then_inc(roots_done, 1)

        @block.vector
        def _(dve):
            V = nc.vector
            links = [0]

            def link(ins):
                links[0] += 1
                ins.then_inc(chain, 1)
                dve.wait_ge(chain, links[0])

            def split_tile(piece, k, tiles_before=None):
                n = piece * KD + k
                slot = k // 2
                raw = ring[:, slot, (k % 2) * PIECE:(k % 2 + 1) * PIECE]
                if k % 2 == 0:
                    dve.wait_ge(unit_loaded[slot], piece * 16 + 16)
                if tiles_before is None or tiles_before + k >= 2:
                    dve.wait_ge(tile_used, n - 1)
                V.tensor_copy(w_hi[:, k % 2, :], raw).then_inc(hi_split, 1)
                dve.wait_ge(hi_split, n + 1)
                V.tensor_tensor(w_lo[:, k % 2, :], raw, w_hi[:, k % 2, :].bitcast(f32), ALU.subtract)\
                 .then_inc(tile_split, 1)

            dve.wait_ge(vecs_ready, 1)
            for g in range(KD // 2):
                b = 4 + g % 4
                dve.wait_ge(x_transposed, g + 1)
                if g >= 2:
                    dve.wait_ge(act_ready, g - 1)
                gain = vec_cols[:, 2 * g:2 * g + 2].unsqueeze(2).to_broadcast([P, 2, SEQ])
                V.tensor_tensor(xg_t[:, g % 2, :, :], bank[b][:, :].rearrange("p (k n) -> p k n", k=2), gain,
                                ALU.mult).then_inc(x_scaled, 1)
                if g >= 1:
                    split_tile(0, 2 * g - 2, tiles_before=0)
                dve.wait_ge(act_hi_ready, g + 1)
                V.tensor_tensor(act_lo[:, 2 * g:2 * g + 2, :], xg_t[:, g % 2, :, :],
                                act_hi[:, 2 * g:2 * g + 2, :].bitcast(f32), ALU.subtract).then_inc(act_ready, 1)
                if g >= 1:
                    split_tile(0, 2 * g - 1, tiles_before=0)
            dve.wait_ge(roots_done, 1)
            V.reciprocal(rinv[:, 0:2], root[:, 0:2]).then_inc(rinv_ready, 1)
            split_tile(0, KD - 2)
            split_tile(0, KD - 1)
            with dve.Fori(1, PIECES_IN) as piece:
                for k in range(KD):
                    split_tile(piece, k)

            dve.wait_ge(roots_done, 2)
            V.reciprocal(rinv[:, 2:4], root[:, 2:4]).then_inc(rinv_ready, 1)
            dve.wait_ge(rinv_ready, 2)
            dve.wait_ge(gain_loaded, 16)
            for b in range(NB):
                V.scalar_tensor_tensor(out=v[:, b, :], in0=v[:, b, :], scalar=rinv[:, 2 + b:3 + b],
                                       in1=gain_bc[:, :], op0=ALU.mult, op1=ALU.mult).then_inc(v_ready, 1)

            dve.wait_ge(z_ready, 16)

            def low_half(h):
                dve.wait_ge(act_hi_ready, KD // 2 + h + 1)
                V.tensor_tensor(act_lo[:, 2 * h:2 * h + 2, :].rearrange("p k n -> p (k n)"), bank[h][:, :],
                                act_hi[:, 2 * h:2 * h + 2, :].rearrange("p k n -> p (k n)").bitcast(f32),
                                ALU.subtract).then_inc(act_ready, 1)

            for h in range(HEADS):
                dve.wait_ge(mixed, h + 1)
                for b in range(NB):
                    last = V.scalar_tensor_tensor(out=u[:, b, h * HD:(h + 1) * HD], in0=bank[h][:, b * HD:(b + 1) * HD],
                                                  scalar=vec_cols[:, 2 * KD + h:2 * KD + h + 1],
                                                  in1=u[:, b, h * HD:(h + 1) * HD], op0=ALU.add, op1=ALU.mult)
                last.then_inc(gated, 1)
                if h >= 2:
                    low_half(h - 2)
            split_tile(PIECES_IN, 0)
            low_half(HEADS - 2)
            low_half(HEADS - 1)
            split_tile(PIECES_IN, 1)

            def add_residual(piece):
                c0 = (piece - PIECES_IN) * PIECE
                dve.wait_ge(tile_used, KD * (piece + 1))
                for c in range(2):
                    for b in range(NB):
                        cols = slice(c0 + c * BANK, c0 + (c + 1) * BANK)
                        V.tensor_tensor(x[:, b, cols], x[:, b, cols],
                                        bank[4 * (piece % 2) + 2 * c + b][:, :], ALU.add).then_inc(h2_ready, 1)

            for k in range(2, KD):
                split_tile(PIECES_IN, k)
            split_tile(PIECES_IN + 1, 0)
            split_tile(PIECES_IN + 1, 1)
            add_residual(PIECES_IN)
            for k in range(2, KD):
                split_tile(PIECES_IN + 1, k)
            add_residual(PIECES_IN + 1)

            dve.wait_ge(sq_done, 4 * NB)
            V.tensor_tensor(ss[:, 4:6], root[:, 0:2], root[:, 2:4], ALU.add).then_inc(rinv_ready, 1)
            dve.wait_ge(router_loaded, 32)
            V.tensor_tensor(rwg[:, :, :], rw[:, :, :],
                            vec_cols[:, KD:2 * KD].unsqueeze(2).to_broadcast([P, KD, E]), ALU.mult)\
             .then_inc(rwg_ready, 1)
            dve.wait_ge(roots_done, 3)
            V.reciprocal(rinv[:, 4:6], root[:, 4:6]).then_inc(rinv_ready, 1)
            dve.wait_ge(rinv_ready, 4)
            dve.wait_ge(consts_ready, 7)

            def wide(t, n=E):
                return t.to_broadcast([P, NB, n])

            dve.wait_ge(logits_done, 1)
            for b in range(NB):
                V.tensor_scalar(logit[:, b, :], bank[4 + b][:, 0:E], rinv[:, 4 + b:5 + b], None, ALU.mult)\
                 .then_inc(chain, 1)
            links[0] += NB
            dve.wait_ge(chain, links[0])
            link(V.tensor_reduce(red[:, :, 0:1], logit[:, :, :], AX.X, ALU.max))
            V.tensor_tensor(shifted[:, :, :], logit[:, :, :], wide(red[:, :, 0:1]), ALU.subtract)\
             .then_inc(shifted_ready, 1)
            dve.wait_ge(exp_done, 1)
            link(V.tensor_reduce(red[:, :, 1:2], expd[:, :, :], AX.X, ALU.add))
            link(V.reciprocal(red[:, :, 2:3], red[:, :, 1:2]))
            link(V.tensor_tensor(probs[:, :, :], expd[:, :, :], wide(red[:, :, 2:3]), ALU.mult))
            link(V.tensor_tensor(sel[:, :, :], probs[:, :, :], rb[:, :, :].to_broadcast([P, NB, E]), ALU.add))

            s4 = sel[:, :, :].rearrange("p b (g k) -> p b g k", g=GROUPS)
            V.tensor_tensor(pairs[:, :, :, 0:2], s4[:, :, :, 0:2], s4[:, :, :, 2:4], ALU.add).then_inc(chain, 1)
            V.tensor_tensor(pairs[:, :, :, 2:4], s4[:, :, :, 0:4:2], s4[:, :, :, 1:4:2], ALU.add).then_inc(chain, 1)
            V.tensor_tensor(pairs[:, :, :, 4:5], s4[:, :, :, 0:1], s4[:, :, :, 3:4], ALU.add).then_inc(chain, 1)
            V.tensor_tensor(pairs[:, :, :, 5:6], s4[:, :, :, 1:2], s4[:, :, :, 2:3], ALU.add).then_inc(chain, 1)
            links[0] += 4
            dve.wait_ge(chain, links[0])
            link(V.tensor_reduce(gscore[:, :, :, :], pairs[:, :, :, :], AX.X, ALU.max))

            def first_best(dst, values, k, weights, n, col):
                link(V.tensor_reduce(red[:, :, col:col + 1], values, AX.X, ALU.max))
                link(V.tensor_tensor(k, values, wide(red[:, :, col:col + 1], n), ALU.is_equal))
                link(V.tensor_tensor(k, k, weights, ALU.mult))
                link(V.tensor_reduce(red[:, :, col + 1:col + 2], k, AX.X, ALU.max))
                link(V.tensor_tensor(dst, k, wide(red[:, :, col + 1:col + 2], n), ALU.is_equal))

            first_best(gpick[:, :, :, 0], gscore[:, :, :, 0], gkey[:, :, :, 0],
                       rev[:, :, E - GROUPS:E].to_broadcast([P, NB, GROUPS]), GROUPS, 3)
            link(V.tensor_scalar(gpen[:, :, :, :], gpick[:, :, :, :], BIG, -BIG, ALU.mult, ALU.add))
            m4 = masked[:, :, :].rearrange("p b (g k) -> p b g k", g=GROUPS)
            spread = [P, NB, GROUPS, PER_GROUP]
            link(V.tensor_tensor(m4, s4, gpick[:, :, :, :].to_broadcast(spread), ALU.mult))
            link(V.tensor_tensor(m4, m4, gpen[:, :, :, :].to_broadcast(spread), ALU.add))
            falling = rev[:, :, :].to_broadcast([P, NB, E])
            first_best(first[:, :, :], masked[:, :, :], key[:, :, :], falling, E, 5)
            link(V.scalar_tensor_tensor(out=masked[:, :, :], in0=first[:, :, :], scalar=-3.0 * BIG,
                                        in1=masked[:, :, :], op0=ALU.mult, op1=ALU.add))
            first_best(assigned[:, :, :], masked[:, :, :], key[:, :, :], falling, E, 7)
            links[0] += 1
            V.tensor_tensor(assigned[:, :, :], assigned[:, :, :], first[:, :, :], ALU.add)\
             .then_inc(assigned_ready, 1)
            links[0] -= 1
            dve.wait_ge(assigned_ready, 1)
            link(V.tensor_tensor(wsel[:, :, :], probs[:, :, :], assigned[:, :, :], ALU.mult))
            link(V.tensor_reduce(red[:, :, 9:10], wsel[:, :, :], AX.X, ALU.add))
            link(V.reciprocal(red[:, :, 10:11], red[:, :, 9:10]))
            link(V.tensor_tensor(weight_of[:, :, 0:E], wsel[:, :, :], wide(red[:, :, 10:11]), ALU.mult))
            dve.wait_ge(ranks_done, 1)
            link(V.scalar_tensor_tensor(out=rank_t[:, :, :], in0=bank[6][:, 0:NB * E].rearrange("p (b e) -> p b e", b=NB),
                                        scalar=FAR, in1=assigned[:, :, :], op0=ALU.add, op1=ALU.mult))
            link(V.tensor_scalar(rank_of[:, :, 0:E], rank_t[:, :, :], -FAR, None, ALU.add))
            for b in range(NB):
                last = V.tensor_scalar(pick[:, b, :], tok_of[:, 0:TOK], rank_of[:, b, 0:1], rinv[:, 4 + b:5 + b],
                                       ALU.is_equal, ALU.mult)
            last.then_inc(pick_ready, 1)

            count = bank[7][:, 0:E]
            link(V.tensor_scalar(extra[:, 0, :], count, TOK + 0.5, None, ALU.is_gt))
            for n in range(2, SEQ // TOK):
                link(V.scalar_tensor_tensor(out=extra[:, 0, :], in0=count, scalar=n * TOK + 0.5,
                                            in1=extra[:, 0, :], op0=ALU.is_gt, op1=ALU.add))
            link(V.tensor_tensor_scan(upto[:, 0, :], ones[:, 0:E], extra[:, 0, :], 0.0, ALU.mult, ALU.add))
            link(V.tensor_tensor(start[:, 0, :], upto[:, 0, :], extra[:, 0, :], ALU.subtract))
            over = [P, MORE, E]
            q_wide = q_idx[:, :, :].to_broadcast(over)
            link(V.tensor_tensor(qa[:, :, :], upto[:, :, :].to_broadcast(over), q_wide, ALU.is_gt))
            link(V.tensor_tensor(qsel[:, :, :], start[:, :, :].to_broadcast(over), q_wide, ALU.is_le))
            link(V.tensor_tensor(qsel[:, :, :], qsel[:, :, :], qa[:, :, :], ALU.mult))
            link(V.tensor_tensor(qoff[:, :, :], start[:, :, :].to_broadcast(over), q_wide, ALU.subtract))
            link(V.tensor_scalar(qoff[:, :, :], qoff[:, :, :], -float(TOK), float(TOK), ALU.mult, ALU.add))
            for b in range(NB):
                link(V.tensor_tensor(qt[:, :, :], rank_of[:, b:b + 1, 0:E].to_broadcast(over), qoff[:, :, :],
                                     ALU.subtract))
                link(V.tensor_tensor(qt[:, :, :], qt[:, :, :], qsel[:, :, :], ALU.mult))
                link(V.tensor_reduce(rank_of[:, b, E:MAX_ITEMS], qt[:, :, :], AX.X, ALU.add))
                link(V.tensor_tensor(qt[:, :, :], weight_of[:, b:b + 1, 0:E].to_broadcast(over), qsel[:, :, :],
                                     ALU.mult))
                link(V.tensor_reduce(weight_of[:, b, E:MAX_ITEMS], qt[:, :, :], AX.X, ALU.add))
            link(V.tensor_tensor(qt[:, :, :], e_idx[:, :, :].to_broadcast(over), qsel[:, :, :], ALU.mult))
            link(V.tensor_reduce(ids_f[:, E:MAX_ITEMS], qt[:, :, :], AX.X, ALU.add))
            link(V.tensor_copy(ids_f[:, 0:E], e_idx[:, 0, :]))
            link(V.tensor_copy(item_expert[:, :], ids_f[:, :]))
            link(V.tensor_scalar(count_f[:, :], upto[:, 0, E - 1:E], float(E), None, ALU.add))
            V.tensor_copy(item_count[:, :], count_f[:, :]).then_inc(tables_ready, 1)

            ffn_gain = [vec_cols[:, KD + 8 * g:KD + 8 * g + 8].unsqueeze(2).to_broadcast([P, 8, TOK])
                        for g in range(2)]

            def take_gathered():
                for g in range(2):
                    last = V.tensor_tensor(xg[:, 8 * g:8 * g + 8, :],
                                           bank[6 + g][:, :].rearrange("p (k t) -> p k t", k=8), ffn_gain[g],
                                           ALU.mult)
                last.then_inc(xg_ready, 1)

            def add_back(scattered_before):
                for j in range(8):
                    b, c = j // 4, j % 4
                    dve.wait_ge(scattered, scattered_before + (j + 1))
                    cols = slice(c * BANK, (c + 1) * BANK)
                    V.tensor_tensor(acc[:, b, cols], acc[:, b, cols], bank[5 + j % 3][:, :], ALU.add)\
                     .then_inc(acc_added, 1)

            dve.wait_ge(gathered, 1)
            take_gathered()
            dve.wait_ge(tables_ready, 1)
            n_items = dve.value_load(item_count[0:1, 0:1], min_val=E, max_val=MAX_ITEMS)
            dve.wait_ge(acc_set, NB)
            with dve.Fori(0, n_items) as i:
                for b in range(NB):
                    V.tensor_scalar(place[:, b, :], tok_of[:, :], rank_of[:, b, bass.ds(i, 1)],
                                    weight_of[:, b, bass.ds(i, 1)], ALU.is_equal, ALU.mult)
                for b in range(NB):
                    last = V.tensor_scalar(pick[:, b, :], tok_of[:, 0:TOK], rank_of[:, b, bass.ds(i + 1, 1)],
                                           rinv[:, 4 + b:5 + b], ALU.is_equal, ALU.mult)
                last.then_inc(pick_ready, 1)
                dve.wait_ge(sil_ready, i * 2 + 1)
                V.tensor_tensor(hid[TOK:P, :], sil[TOK:P, :], bank[0][TOK:P, :], ALU.mult)
                dve.wait_ge(sil_ready, i * 2 + 2)
                V.tensor_tensor(hid[0:TOK, :], sil[0:TOK, :], bank[1][0:TOK, :], ALU.mult).then_inc(hid_ready, 1)
                add_back(i * 8)
                dve.wait_ge(gathered, i + 2)
                take_gathered()
            add_back(n_items * 8)

            dve.wait_ge(roots_done, 4)
            V.reciprocal(rinv[:, 6:8], root[:, 6:8]).then_inc(rinv_ready, 1)
            dve.wait_ge(rinv_ready, 5)
            dve.wait_ge(gain_loaded, 32)
            for n in range(2 * NB):
                b, c = n // 2, n % 2 * PIECE
                V.scalar_tensor_tensor(out=acc[:, b, c:c + PIECE], in0=acc[:, b, c:c + PIECE],
                                       scalar=rinv[:, 6 + b:7 + b], in1=gain_bc[:, c:c + PIECE],
                                       op0=ALU.mult, op1=ALU.mult).then_inc(out_ready, 1)

        @block.tensor
        def _(pe):
            T = nc.tensor
            pe.wait_ge(ident_ready, 1)
            pe.wait_ge(vecs_loaded, 48)
            rows = 2 * KD + HEADS
            T.transpose(bank[0][:, 0:rows], vec_raw, ident[0:rows, 0:rows]).then_inc(vecs_transposed, 1)

            def transpose_pair(dst, src, g):
                for s in range(2):
                    for b in range(NB):
                        k = 2 * g + s
                        last = T.transpose(dst[:, s * SEQ + b * P:s * SEQ + (b + 1) * P],
                                           src[:, b, k * P:(k + 1) * P], ident[:, :])
                return last

            pe.wait_ge(x_loaded[0], 16)
            pe.wait_ge(x_loaded[1], 16)
            for g in range(4):
                transpose_pair(bank[4 + g], x, g).then_inc(x_transposed, 1)

            def project_slab(bank_set, k):
                last = None
                for c in range(2):
                    for b in range(NB):
                        dst = bank[4 * bank_set + 2 * c + b][:, :]
                        hi, lo = (t[:, k, b * P:(b + 1) * P] for t in (act_hi, act_lo))
                        wh, wl = (t[:, k % 2, c * BANK:(c + 1) * BANK] for t in (w_hi, w_lo))
                        T.matmul(dst, hi, wh, start=(k == 0), stop=False)
                        T.matmul(dst, hi, wl, start=False, stop=False)
                        last = T.matmul(dst, lo, wh, start=False, stop=(k == KD - 1))
                last.then_inc(tile_used, 1)

            pe.wait_ge(vecs_ready, 1)
            for k in range(KD):
                if k % 2 == 0 and 2 <= k < 10:
                    g = k // 2 + 3
                    pe.wait_ge(x_scaled, g - 3)
                    transpose_pair(bank[4 + g % 4], x, g).then_inc(x_transposed, 1)
                if k == 12:
                    pe.wait_ge(ws_masked, 1)
                    for g in range(2):
                        pe.wait_ge(x_scaled, 5 + g)
                        for h in range(4):
                            last = T.transpose(bank[4 + g][:, h * P:(h + 1) * P], ws_raw[:, 4 * g + h, :],
                                               ident[:, :])
                        last.then_inc(ws_transposed, 1)
                if k % 2 == 0:
                    pe.wait_ge(act_ready, k // 2 + 1)
                pe.wait_ge(tile_split, k + 1)
                project_slab(0, k)
            pe.wait_ge(x_scaled, KD // 2)
            pe.wait_ge(ws_ready, 2)
            for k in range(KD):
                pe.wait_ge(tile_split, KD + k + 1)
                project_slab(1, k)
            for piece in range(2, PIECES_IN):
                pe.wait_ge(z_ready, 4 * (piece - 1))
                for k in range(KD):
                    pe.wait_ge(tile_split, KD * piece + k + 1)
                    project_slab(piece % 2, k)

            pe.wait_ge(v_ready, NB)
            for h in range(HEADS):
                if h % 4 == 0:
                    pe.wait_ge(z_ready, 12 + h)
                for b in range(NB):
                    last = T.matmul(bank[h][:, b * HD:(b + 1) * HD], ws_t[:, h, :], v[:, b, h * HD:(h + 1) * HD],
                                    start=True, stop=True)
                last.then_inc(mixed, 1)
            for h in range(HEADS):
                pe.wait_ge(gated, h + 1)
                transpose_pair(bank[h], u, h).then_inc(gated_t, 1)

            for piece in range(PIECES_IN, PIECES):
                pe.wait_ge(act_ready, KD // 2 + 4 * (piece - PIECES_IN + 1))
                for k in range(KD):
                    if piece == PIECES_IN and k >= 8 and k % 2 == 0:
                        pe.wait_ge(act_ready, KD // 2 + k // 2 + 1)
                    pe.wait_ge(tile_split, KD * piece + k + 1)
                    project_slab(piece % 2, k)
                    if piece == PIECES_IN + 1 and k == 7:
                        pe.wait_ge(h2_ready, 4)
                        for g in range(4):
                            transpose_pair(bank[g], x, g).then_inc(h2_transposed, 1)
            for g in range(4):
                if g == 0:
                    pe.wait_ge(h2_ready, 6)
                    pe.wait_ge(h2_t_ready, 4)
                if g == 2:
                    pe.wait_ge(h2_ready, 8)
                transpose_pair(bank[g], x, 4 + g).then_inc(h2_transposed, 1)

            pe.wait_ge(rwg_ready, 1)
            for k in range(KD):
                if k >= 8 and k % 2 == 0:
                    pe.wait_ge(h2_t_ready, k // 2 + 1)
                for b in range(NB):
                    last = T.matmul(bank[4 + b][:, 0:E], h2_t[:, k, b * P:(b + 1) * P], rwg[:, k, :],
                                    start=(k == 0), stop=(k == KD - 1))
            last.then_inc(logits_done, 1)
            pe.wait_ge(assigned_ready, 1)
            flat = assigned[:, :, :].rearrange("p b e -> p (b e)")
            T.matmul(bank[6][:, 0:NB * E], before[:, :], flat, start=True, stop=False)
            T.matmul(bank[6][:, E:2 * E], ones[:, :], assigned[:, 0, :], start=False, stop=True)
            for b in range(NB):
                last = T.matmul(bank[7][:, 0:E], ones[:, :], assigned[:, b, :], start=(b == 0), stop=(b == NB - 1))
            last.then_inc(ranks_done, 1)

            def gather():
                for k in range(KD):
                    for b in range(NB):
                        last = T.matmul(bank[6 + k // 8][:, k % 8 * TOK:(k % 8 + 1) * TOK],
                                        x[:, b, k * P:(k + 1) * P], pick[:, b, :], start=(b == 0), stop=(b == NB - 1))
                last.then_inc(gathered, 1)

            def scatter(added_before):
                for j in range(8):
                    b, jj, h = j // 4, j % 4 // 2, j % 2
                    if j >= 3:
                        pe.wait_ge(acc_added, added_before + (j - 2))
                    T.matmul(bank[5 + j % 3][:, :], back[h * TOK:(h + 1) * TOK, b * P:(b + 1) * P],
                             y[h * TOK:(h + 1) * TOK, jj, :], start=True, stop=True).then_inc(scattered, 1)

            pe.wait_ge(tables_ready, 1)
            pe.wait_ge(pick_ready, 1)
            gather()
            n_items = pe.value_load(item_count[0:1, 0:1], min_val=E, max_val=MAX_ITEMS)
            with pe.Fori(0, n_items) as i:
                pe.wait_ge(xg_ready, i + 1)
                for m in range(PIECE_UNITS):
                    for unit in (2 * m, 2 * m + 1):
                        pe.wait_ge(unit_loaded[slot_of(unit)], i * 32 + 16 * loads_before(unit))
                    for s in range(2):
                        for c in range(2):
                            for up in range(2):
                                at = TOK * ((up + c) % 2)
                                last = T.matmul(bank[c][at:at + TOK, :], xg[:, 2 * m + s, :],
                                                ring[:, slot_of(2 * m + up), s * F + c * BANK:s * F + (c + 1) * BANK],
                                                start=(m == 0 and s == 0), stop=(m == PIECE_UNITS - 1 and s == 1))
                    last.then_inc(step_done, 1)
                pe.wait_ge(y_ready, i + 1)
                pe.wait_ge(back_ready, i + 1)
                scatter(i * 8)
                pe.wait_ge(acc_added, i * 8 + 8)
                pe.wait_ge(pick_ready, i + 2)
                for b in range(NB):
                    last = T.transpose(bank[5][:, b * P:(b + 1) * P], place[:, b, :], ident[:, :])
                last.then_inc(place_transposed, 1)
                gather()
                pe.wait_ge(hid_ready, i + 1)
                for f in range(4):
                    last = T.transpose(bank[4][:, f * P:(f + 1) * P], hid[:, f * P:(f + 1) * P], ident[:, :])
                last.then_inc(hid_transposed, 1)
                pe.wait_ge(hid_t_ready, i + 1)
                for f in range(KF):
                    unit = 2 * PIECE_UNITS + f
                    pe.wait_ge(unit_loaded[slot_of(unit)], i * 32 + 16 * loads_before(unit))
                    hidden = hid_t[:, f % 4, TOK:P] if f < 4 else hid_t[:, f % 4, 0:TOK]
                    for c in range(4):
                        at = TOK * (c % 2)
                        last = T.matmul(bank[2 + c // 2][at:at + TOK, :], hidden,
                                        ring[:, slot_of(unit), c * BANK:(c + 1) * BANK],
                                        start=(f == 0), stop=(f == KF - 1))
                    last.then_inc(step_done, 1)
            pe.wait_ge(xg_ready, n_items + 1)
            pe.wait_ge(y_ready, n_items + 1)
            pe.wait_ge(back_ready, n_items + 1)
            scatter(n_items * 8)


_INS = ['x', 'norm_mix_g', 'norm_ffn_g', 'final_g', 'a_w_in', 'a_v_gain', 'a_w_s', 'a_b_s', 'a_w_out',
        'router_w', 'router_b', 'moe_w_gate', 'moe_w_up', 'moe_w_down']


def kernel(**inputs):
    import numpy as np
    import concourse.bacc as bacc
    from concourse.bass_utils import run_bass_kernel_spmd

    nc = bacc.Bacc("TRN2", target_bir_lowering=False, num_devices=1)
    arrays, args = {}, []
    for name in _INS:
        a = np.ascontiguousarray(inputs[name])
        arrays[f"in_{name}"] = a
        args.append(nc.dram_tensor(f"in_{name}", a.shape, mybir.dt.from_np(a.dtype), kind="ExternalInput").ap())
    shape = inputs['x'].shape
    args.append(nc.dram_tensor("out", shape, mybir.dt.float32, kind="ExternalOutput").ap())
    hybrid_trunk_kernel(nc, *args)
    r = run_bass_kernel_spmd(nc, [arrays], core_ids=[0])
    return r.results[0]["out"]
```

```python
import concourse.bass as bass
from concourse import mybir
from contextlib import ExitStack


def hybrid_trunk_kernel(nc, x_in, norm_mix_g, norm_ffn_g, final_g, a_w_in, a_v_gain, a_w_s, a_b_s,
                        a_w_out, router_w, router_b, w_gate, w_up, w_down, out):
    f32, f32r, bf16, i32 = mybir.dt.float32, mybir.dt.float32r, mybir.dt.bfloat16, mybir.dt.int32
    ALU = mybir.AluOpType
    ACT = mybir.ActivationFunctionType
    AX = mybir.AxisListType

    P = 128
    SEQ, D = x_in.shape[1], x_in.shape[2]
    NB = SEQ // P
    KD = D // P
    HEADS, CHUNK = a_w_s.shape[1], a_w_s.shape[2]
    HD = D // HEADS
    E, F = w_gate.shape[1], w_gate.shape[3]
    GROUPS = 4
    PER_GROUP = E // GROUPS
    TOK = 64
    BANK = 512
    PIECE = 1024
    RING = 12
    SLOTS = 17
    PIECE_UNITS = KD // 2
    PIECES_IN, PIECES_OUT = 2 * D // PIECE, D // PIECE
    PIECES = PIECES_IN + PIECES_OUT
    REUSE = 12
    ITEM_UNITS = 24
    STEPS = 16
    KF = F // P
    MORE = 8
    MAX_ITEMS = E + MORE
    RMS_EPS = 1e-6
    BIG = 1e30
    TINY = 1.2e-38
    QUAD = 32
    SET_OF = [0, 1, 0, 1, 1, 0]
    FAR = 1000.0

    with ExitStack() as ctx:
        def sb(name, shape, dt=f32, at=ctx):
            return at.enter_context(nc.sbuf_tensor(name, shape, dt))

        def sem(name):
            return ctx.enter_context(nc.semaphore(name))

        ring = sb("ring", [P, RING, 2048])
        x = sb("x", [P, NB, D])
        gain_bc = sb("gain_bc", [P, D])
        ident = sb("ident", [P, P])
        vec_cols = sb("vec_cols", [P, 2 * KD + HEADS])
        rw = sb("rw", [P, KD, E])
        rb = sb("rb", [P, 1, E])
        eps = sb("eps", [P, 2])
        ss = sb("ss", [P, 8])
        root = sb("root", [P, 8])
        rinv = sb("rinv", [P, 8])

        mix = ExitStack()
        z = sb("z", [P, 2, NB, D], at=mix)
        ws_t = sb("ws_t", [P, HEADS, CHUNK], at=mix)
        act_hi = sb("act_hi", [P, KD, SEQ], f32r, at=mix)
        act_lo = sb("act_lo", [P, KD, SEQ], f32r, at=mix)
        w_hi = sb("w_hi", [P, 2, PIECE], f32r, at=mix)
        w_lo = sb("w_lo", [P, 2, PIECE], f32r, at=mix)
        v, u = z[:, 0, :, :], z[:, 1, :, :]
        scratch = z[:, 1, :, :].rearrange("p n d -> p (n d)")
        ws_raw = scratch[:, 0:HEADS * CHUNK].rearrange("p (h s) -> p h s", h=HEADS)
        xg_t = scratch[:, 1024:2048].rearrange("p (b k n) -> p b k n", b=2, k=2)
        vec_raw = scratch[0:2 * KD + HEADS, 2048:2176]
        mix.close()

        routing = ExitStack()
        h2_t = sb("h2_t", [P, KD, SEQ], at=routing)
        routing.close()
        x_row = sb("x_row", [P, 2, BANK])
        xg = sb("xg", [P, KD, TOK])
        sil = sb("sil", [P, BANK])
        hid = sb("hid", [P, BANK])
        hid_t = sb("hid_t", [P, 4, 2 * TOK])
        quarter = sb("quarter", [P, SEQ])
        place = sb("place", [P, NB, 2 * TOK])
        acc = sb("acc", [P, NB, D])
        before = sb("before", [P, P], bf16)
        ones = sb("ones", [P, P], bf16)
        ones_row = sb("ones_row", [P, E])
        q_i = sb("q_i", [P, MORE], i32)
        q_idx = sb("q_idx", [P, MORE, 1])
        fold = sb("fold", [P, E])
        rwg = sb("rwg", [P, KD, QUAD])
        tok_of = sb("tok_of", [P, 2 * TOK])
        tok_i = sb("tok_i", [P, 2 * TOK], i32)
        e_idx = sb("e_idx", [P, 1, E])
        e_i = sb("e_i", [P, E], i32)
        later_i = sb("later_i", [P, PER_GROUP, PER_GROUP], i32)
        wins_from = sb("wins_from", [P, 1, PER_GROUP, PER_GROUP])
        y = sb("y", [P, 2, BANK])
        back = sb("back", [P, SEQ])
        pick = sb("pick", [P, NB, TOK])
        expd = sb("expd", [P, NB, E])
        sel = sb("sel", [P, NB * GROUPS, PER_GROUP])
        red = sb("red", [P, NB, 8])
        diff = sb("diff", [P, NB * GROUPS, PER_GROUP, PER_GROUP])
        beaten = sb("beaten", [P, NB * GROUPS, PER_GROUP])
        top_sel = sb("top_sel", [P, NB * GROUPS, PER_GROUP])
        gscore = sb("gscore", [P, NB, GROUPS])
        gdiff = sb("gdiff", [P, NB, GROUPS, GROUPS])
        gbeaten = sb("gbeaten", [P, NB * GROUPS, 1])
        gpick = sb("gpick", [P, NB * GROUPS, 1])
        assigned = sb("assigned", [P, NB, E], bf16)
        wsel = sb("wsel", [P, NB, E])
        rank_t = sb("rank_t", [P, NB, E])
        extra = sb("extra", [P, 1, E])
        upto = sb("upto", [P, 1, E])
        start = sb("start", [P, 1, E])
        qa = sb("qa", [P, MORE, E])
        qsel = sb("qsel", [P, MORE, E])
        qoff = sb("qoff", [P, MORE, E])
        qt = sb("qt", [P, MORE, E])
        rank_of = sb("rank_of", [P, NB, MAX_ITEMS + 2])
        weight_of = sb("weight_of", [P, NB, MAX_ITEMS + 2])
        more_slots = sb("more_slots", [P, SLOTS - RING, 2048])
        ids_f = sb("ids_f", [P, MAX_ITEMS])
        item_expert = sb("item_expert", [P, MAX_ITEMS], i32)
        last_index = sb("last_index", [P, 1], i32)

        bank = [ctx.enter_context(nc.psum_tensor(f"bank{b}", [P, BANK], f32)) for b in range(8)]

        x_loaded = [sem(f"x_loaded{b}") for b in range(4)]
        vecs_loaded = sem("vecs_loaded")
        ws_loaded = sem("ws_loaded")
        router_loaded = sem("router_loaded")
        gain_loaded = sem("gain_loaded")
        unit_loaded = [sem(f"unit_loaded{s}") for s in range(SLOTS)]
        ident_ready = sem("ident_ready")
        ws_masked = sem("ws_masked")
        vecs_transposed = sem("vecs_transposed")
        vecs_ready = sem("vecs_ready")
        x_transposed = sem("x_transposed")
        x_scaled = sem("x_scaled")
        act_hi_ready = sem("act_hi_ready")
        act_ready = sem("act_ready")
        ws_transposed = sem("ws_transposed")
        ws_ready = sem("ws_ready")
        hi_split = sem("hi_split")
        tile_split = sem("tile_split")
        tile_used = sem("tile_used")
        sq_done = sem("sq_done")
        sq_v_done = sem("sq_v_done")
        roots_done = sem("roots_done")
        rinv_ready = sem("rinv_ready")
        z_ready = sem("z_ready")
        v_ready = sem("v_ready")
        mixed = sem("mixed")
        gated = sem("gated")
        gated_t = sem("gated_t")
        h2_ready = sem("h2_ready")
        h2_transposed = sem("h2_transposed")
        h2_t_ready = sem("h2_t_ready")
        consts_ready = sem("consts_ready")
        pool_step = sem("pool_step")
        rwg_ready = sem("rwg_ready")
        logits_done = sem("logits_done")
        quarters_done = sem("quarters_done")
        quarter_ready = sem("quarter_ready")
        shift_ready = sem("shift_ready")
        exp_done = sem("exp_done")
        assigned_ready = sem("assigned_ready")
        ranks_done = sem("ranks_done")
        count_ready = sem("count_ready")
        tables_ready = sem("tables_ready")
        row_a_ready = sem("row_a_ready")
        row_b_ready = sem("row_b_ready")
        row_transposed = sem("row_transposed")
        chain = sem("chain")
        acc_set = sem("acc_set")
        pick_ready = sem("pick_ready")
        place_ready = sem("place_ready")
        gathered = sem("gathered")
        xg_ready = sem("xg_ready")
        step_done = sem("step_done")
        sil_ready = sem("sil_ready")
        hid_ready = sem("hid_ready")
        hid_transposed = sem("hid_transposed")
        hid_t_ready = sem("hid_t_ready")
        y_ready = sem("y_ready")
        last_y_ready = sem("last_y_ready")
        place_transposed = sem("place_transposed")
        back_ready = sem("back_ready")
        scattered = sem("scattered")
        acc_added = sem("acc_added")
        out_ready = sem("out_ready")
        stored = sem("stored")

        w_in_v = a_w_in[0].rearrange("(k p) c -> p k c", p=P)
        w_out_v = a_w_out[0].rearrange("(k p) c -> p k c", p=P)
        gate_v = w_gate[0].rearrange("e (k p) c -> p e k c", p=P)
        up_v = w_up[0].rearrange("e (k p) c -> p e k c", p=P)
        down_v = w_down[0].rearrange("e (k p) c -> p e k c", p=P)
        x_v = x_in[0].rearrange("(b p) d -> p b d", p=P)
        out_v = out[0].rearrange("(b p) d -> p b d", p=P)

        def slot_of(unit):
            if unit >= SLOTS:
                unit -= REUSE
            return unit + PIECE_UNITS if unit < RING - PIECE_UNITS else unit - 4 if unit < RING else unit

        def shared(unit):
            return SLOTS - REUSE <= unit < ITEM_UNITS - REUSE or unit >= SLOTS

        def slot(s):
            return ring[:, s, :] if s < RING else more_slots[:, s - RING, :]

        def unit_count(i, unit):
            mixer = PIECES if slot_of(unit) < PIECE_UNITS else 0
            return i * (32 if shared(unit) else 16) + 16 * (mixer + (2 if unit >= SLOTS else 1))

        def step_of(unit):
            return unit // 2 if unit < 2 * PIECE_UNITS else unit - PIECE_UNITS

        block = ctx.enter_context(nc.Block())

        @block.sync
        def _(sp):
            sp.dma_start(vec_raw[0:KD, :], norm_mix_g[0].rearrange("(k p) -> k p", p=P)).then_inc(vecs_loaded, 16)
            sp.dma_start(vec_raw[KD:2 * KD, :], norm_ffn_g[0].rearrange("(k p) -> k p", p=P)).then_inc(vecs_loaded, 16)
            sp.dma_start(vec_raw[2 * KD:2 * KD + HEADS, :], a_b_s[0]).then_inc(vecs_loaded, 16)

            def load_x(c):
                cols = slice(c * BANK, (c + 1) * BANK)
                sp.dma_start(x[:, :, cols], x_v[:, :, cols]).then_inc(x_loaded[c], 16)

            load_x(0)
            for p in range(PIECES):
                for j in range(PIECE_UNITS):
                    if p >= 1:
                        sp.wait_ge(tile_split, KD * (p - 1) + 2 * j + 2)
                    if p < PIECES_IN:
                        c = ((p + 2) % PIECES_IN) * PIECE
                        src = w_in_v[:, 2 * j:2 * j + 2, c:c + PIECE]
                    else:
                        c = (p - PIECES_IN) * PIECE
                        src = w_out_v[:, 2 * j:2 * j + 2, c:c + PIECE]
                    sp.dma_start(ring[:, j, :].rearrange("p (k c) -> p k c", k=2), src)\
                      .then_inc(unit_loaded[j], 16)
                    if p == 0 and j < 3:
                        load_x(j + 1)
                if p == PIECES_IN:
                    sp.wait_ge(v_ready, NB)
                    sp.dma_start(gain_bc[:, :], final_g.rearrange("(a d) -> a d", a=1).to_broadcast([P, D]))\
                      .then_inc(gain_loaded, 16)

            def load_unit(expert, unit):
                dst = slot(slot_of(unit))
                if unit < 2 * PIECE_UNITS:
                    m, w = unit // 2, (gate_v, up_v)[unit % 2]
                    src = w[:, expert, 2 * m:2 * m + 2, :]
                    dst = dst.rearrange("p (k c) -> p k c", k=2)
                    if not isinstance(expert, int):
                        dst = dst.unsqueeze(1)
                else:
                    src = down_v[:, expert, unit - 2 * PIECE_UNITS, :]
                    if not isinstance(expert, int):
                        dst = dst.unsqueeze(1)
                sp.dma_start(dst, src).then_inc(unit_loaded[slot_of(unit)], 16)

            for unit in range(ITEM_UNITS):
                if unit >= SLOTS:
                    sp.wait_ge(step_done, step_of(unit - REUSE) + 1)
                elif unit == RING:
                    sp.wait_ge(tile_used, KD * PIECES)
                elif RING - PIECE_UNITS <= unit < RING:
                    sp.wait_ge(tile_split, KD * (PIECES - 1) + 2 * slot_of(unit) + 2)
                load_unit(0, unit)

            sp.wait_ge(tables_ready, 1)
            last_item = sp.value_load(last_index[0:1, 0:1], min_val=E - 1, max_val=MAX_ITEMS - 1)
            with sp.Fori(1, last_item + 1) as i:
                expert = bass.ds(sp.value_load(item_expert[0:1, bass.ds(i, 1)], min_val=0, max_val=E - 1), 1)
                for unit in range(ITEM_UNITS):
                    if unit >= SLOTS:
                        sp.wait_ge(step_done, i * STEPS + (step_of(unit - REUSE) + 1))
                    elif shared(unit):
                        sp.wait_ge(step_done, i * STEPS + (step_of(unit + REUSE) + 1 - STEPS))
                    else:
                        sp.wait_ge(step_done, i * STEPS + (step_of(unit) + 1 - STEPS))
                    load_unit(expert, unit)

            for n in range(2 * NB):
                b, c = n // 2, n % 2 * PIECE
                sp.wait_ge(out_ready, n + 1)
                sp.dma_start(out_v[:, b, c:c + PIECE], acc[:, b, c:c + PIECE]).then_inc(stored, 16)
            sp.wait_ge(stored, 16 * 2 * NB)

        @block.gpsimd
        def _(pool):
            nc.gpsimd.memset(ident[:, :], 0.0).then_inc(pool_step, 1)
            nc.gpsimd.memset(eps[:, :], RMS_EPS).then_inc(pool_step, 1)
            pool.wait_ge(pool_step, 2)
            nc.gpsimd.affine_select(out=ident[:, :], in_=ident[:, :], compare_op=ALU.not_equal, fill=1.0,
                                    base=0, pattern=[[-1, P]], channel_multiplier=1).then_inc(ident_ready, 1)
            pool.wait_ge(ws_loaded, 16)
            nc.gpsimd.affine_select(out=ws_raw, in_=ws_raw, compare_op=ALU.is_ge, fill=0.0, base=0,
                                    pattern=[[0, HEADS], [-1, CHUNK]], channel_multiplier=1).then_inc(ws_masked, 1)
            pool.wait_ge(mixed, HEADS)
            nc.gpsimd.memset(rwg[:, :, :], 0.0).then_inc(consts_ready, 1)
            nc.gpsimd.memset(ones[:, :], 1.0).then_inc(pool_step, 1)
            nc.gpsimd.memset(ones_row[:, :], 1.0).then_inc(pool_step, 1)
            nc.gpsimd.memset(before[:, :], 1.0).then_inc(pool_step, 1)
            nc.gpsimd.iota(tok_i[:, :], pattern=[[0, 2], [1, TOK]], base=0, channel_multiplier=0).then_inc(pool_step, 1)
            nc.gpsimd.iota(e_i[:, :], pattern=[[1, E]], base=0, channel_multiplier=0).then_inc(pool_step, 1)
            nc.gpsimd.iota(later_i[:, :, :], pattern=[[-1, PER_GROUP], [1, PER_GROUP]], base=0,
                           channel_multiplier=0).then_inc(pool_step, 1)
            nc.gpsimd.iota(q_i[:, :], pattern=[[1, MORE]], base=0, channel_multiplier=0).then_inc(pool_step, 1)
            pool.wait_ge(pool_step, 9)
            nc.gpsimd.affine_select(out=before[:, :], in_=before[:, :], compare_op=ALU.is_gt, fill=0.0, base=0,
                                    pattern=[[1, P]], channel_multiplier=-1).then_inc(consts_ready, 1)
            nc.gpsimd.tensor_copy(tok_of[:, :], tok_i[:, :]).then_inc(consts_ready, 1)
            nc.gpsimd.tensor_copy(e_idx[:, 0, :], e_i[:, :]).then_inc(consts_ready, 1)
            nc.gpsimd.tensor_scalar(wins_from[:, 0, :, :], later_i[:, :, :], 0.0, -TINY, ALU.is_lt, ALU.mult)\
              .then_inc(consts_ready, 1)
            nc.gpsimd.tensor_copy(q_idx[:, :, 0], q_i[:, :]).then_inc(consts_ready, 1)
            pool.wait_ge(tile_used, KD * PIECES)
            nc.gpsimd.memset(rank_of[:, :, :], -FAR).then_inc(consts_ready, 1)
            nc.gpsimd.memset(weight_of[:, :, :], 0.0).then_inc(consts_ready, 1)
            nc.gpsimd.memset(y[:, :, :], 0.0).then_inc(y_ready, 1)
            nc.gpsimd.memset(back[:, :], 0.0).then_inc(back_ready, 1)

        @block.scalar
        def _(act):
            act.wait_ge(vecs_transposed, 1)
            nc.scalar.copy(vec_cols[:, :], bank[0][:, 0:2 * KD + HEADS]).then_inc(vecs_ready, 1)
            for g in range(KD // 2):
                act.wait_ge(x_scaled, g + 1)
                nc.scalar.copy(act_hi[:, 2 * g:2 * g + 2, :], xg_t[:, g % 2, :, :]).then_inc(act_hi_ready, 1)
                if g == 2:
                    act.dma_start(ws_raw, a_w_s[0].rearrange("h t s -> t h s")).then_inc(ws_loaded, 16)
                    act.dma_start(gain_bc[:, :], a_v_gain.to_broadcast([P, D])).then_inc(gain_loaded, 16)
                    act.dma_start(rw[:, :, :], router_w.rearrange("(k p) e -> p k e", p=P)).then_inc(router_loaded, 16)
                    act.dma_start(rb[:, 0, :], router_b.rearrange("(a e) -> a e", a=1).to_broadcast([P, E]))\
                       .then_inc(router_loaded, 16)
            for g in range(2):
                act.wait_ge(ws_transposed, g + 1)
                nc.scalar.copy(ws_t[:, 4 * g:4 * g + 4, :].rearrange("p h s -> p (h s)"), bank[4 + g][:, :])\
                  .then_inc(ws_ready, 1)
            for c in range(4):
                act.wait_ge(x_loaded[c], 16)
            for b in range(NB):
                nc.scalar.activation(v[:, b, :], x[:, b, :], ACT.Square, accum_out=ss[:, b:b + 1]).then_inc(sq_done, 1)
            act.wait_ge(sq_done, NB)
            nc.scalar.activation(root[:, 0:2], ss[:, 0:2], ACT.Sqrt, bias=eps[:, 0:1], scale=1.0 / D)\
              .then_inc(roots_done, 1)

            def gelu_piece(p):
                half, c0 = p // 2, p % 2 * PIECE
                act.wait_ge(tile_used, KD * (p + 1))
                for c in range(2):
                    for b in range(NB):
                        last = nc.scalar.activation(z[:, half, b, c0 + c * BANK:c0 + (c + 1) * BANK],
                                                    bank[4 * (p % 2) + 2 * c + b][:, :], ACT.Gelu_apprx_tanh,
                                                    scale=rinv[:, b:b + 1])
                        last.then_inc(z_ready, 1)

            act.wait_ge(rinv_ready, 1)
            gelu_piece(0)
            gelu_piece(1)
            act.wait_ge(z_ready, 8)
            for b in range(NB):
                nc.scalar.activation(u[:, b, :], v[:, b, :], ACT.Square, accum_out=ss[:, 2 + b:3 + b])\
                  .then_inc(sq_done, 1)
            act.wait_ge(sq_done, 2 * NB)
            nc.scalar.activation(root[:, 2:4], ss[:, 2:4], ACT.Sqrt, bias=eps[:, 0:1], scale=1.0 / D)\
              .then_inc(roots_done, 1)
            gelu_piece(2)

            def high_halves(heads):
                for h in heads:
                    act.wait_ge(gated_t, h + 1)
                    nc.scalar.copy(act_hi[:, 2 * h:2 * h + 2, :].rearrange("p k n -> p (k n)"), bank[h % 4][:, :])\
                      .then_inc(act_hi_ready, 1)

            high_halves(range(4))
            gelu_piece(3)
            high_halves(range(4, HEADS))

            def h2_by_features(half):
                for g in range(4 * half, 4 * half + 4):
                    act.wait_ge(h2_transposed, g + 1)
                    nc.scalar.copy(h2_t[:, 2 * g:2 * g + 2, :].rearrange("p k n -> p (k n)"), bank[4 + g % 4][:, :])\
                      .then_inc(h2_t_ready, 1)

            h2_by_features(0)
            for b in range(NB):
                nc.scalar.activation(acc[:, b, 0:PIECE], x[:, b, 0:PIECE], ACT.Square,
                                     accum_out=ss[:, 4 + b:5 + b]).then_inc(sq_done, 1)
            nc.scalar.activation(eps[:, 1:2], eps[:, 0:1], ACT.Sqrt)
            h2_by_features(1)
            act.wait_ge(sq_v_done, NB)
            nc.scalar.activation(root[:, 4:6], ss[:, 6:8], ACT.Sqrt, bias=eps[:, 0:1], scale=1.0 / D)\
              .then_inc(roots_done, 1)
            act.wait_ge(quarters_done, 1)
            nc.scalar.copy(quarter[:, :], bank[0][:, 0:SEQ]).then_inc(quarter_ready, 1)
            act.wait_ge(shift_ready, 1)
            for b in range(NB):
                nc.scalar.activation(expd[:, b, :], bank[1][:, b * E:(b + 1) * E], ACT.Exp, scale=rinv[:, 4 + b:5 + b],
                                     bias=red[:, b, 1:2], accum_out=red[:, b, 2:3]).then_inc(exp_done, 1)
            act.wait_ge(gathered, 1)
            nc.scalar.copy(x_row[:, 0, :], bank[6][:, :]).then_inc(row_a_ready, 1)
            for b in range(NB):
                nc.scalar.copy(acc[:, b, :], x[:, b, :]).then_inc(acc_set, 1)

            act.wait_ge(count_ready, 1)
            last_item = act.value_load(last_index[0:1, 0:1], min_val=E - 1, max_val=MAX_ITEMS - 1)

            def item(i, last=False):
                act.wait_ge(step_done, i * STEPS + STEPS // 2)
                nc.scalar.activation(sil[TOK:P, :], bank[0][0:TOK, :], ACT.Silu).then_inc(sil_ready, 1)
                nc.scalar.activation(sil[0:TOK, :], bank[1][TOK:P, :], ACT.Silu).then_inc(sil_ready, 1)
                act.wait_ge(place_transposed, i + 1)
                nc.scalar.copy(back[:, :], bank[5][:, 0:SEQ]).then_inc(back_ready, 1)
                if not last:
                    act.wait_ge(gathered, i + 2)
                    nc.scalar.copy(x_row[:, 0, :], bank[6][:, :]).then_inc(row_a_ready, 1)
                act.wait_ge(hid_transposed, i + 1)
                nc.scalar.copy(hid_t[:, :, :].rearrange("p f t -> p (f t)"), bank[4][:, :]).then_inc(hid_t_ready, 1)
                act.wait_ge(step_done, i * STEPS + STEPS)
                if last:
                    nc.scalar.copy(y[:, 0, :], bank[2][:, :]).then_inc(y_ready, 1)
                else:
                    nc.scalar.copy(y[:, 0, :], bank[2][:, :])
                    nc.scalar.copy(y[:, 1, :], bank[3][:, :]).then_inc(y_ready, 1)

            with act.Fori(0, last_item) as i:
                item(i)
            item(last_item, last=True)

            nc.scalar.activation(eps[:, 1:2], eps[:, 0:1], ACT.Sqrt)
            act.wait_ge(acc_added, last_item * 8 + 12)
            nc.scalar.activation(x[:, 0, :], acc[:, 0, :], ACT.Square, accum_out=ss[:, 4:5]).then_inc(sq_done, 1)
            act.wait_ge(acc_added, last_item * 8 + 14)
            nc.scalar.activation(x[:, 1, 0:PIECE], acc[:, 1, 0:PIECE], ACT.Square, accum_out=ss[:, 5:6])\
              .then_inc(sq_done, 1)
            act.wait_ge(sq_done, 3 * NB + 2)
            nc.scalar.activation(root[:, 4:5], ss[:, 4:5], ACT.Sqrt, bias=eps[:, 0:1], scale=1.0 / D)\
              .then_inc(roots_done, 1)
            act.wait_ge(sq_v_done, NB + 1)
            nc.scalar.activation(root[:, 5:6], ss[:, 6:7], ACT.Sqrt, bias=eps[:, 0:1], scale=1.0 / D)\
              .then_inc(roots_done, 1)

        @block.vector
        def _(dve):
            V = nc.vector
            links = [0]

            def link(ins):
                links[0] += 1
                ins.then_inc(chain, 1)
                dve.wait_ge(chain, links[0])

            def split_tile(piece, k, tiles_before=None):
                n = piece * KD + k
                slot = k // 2
                raw = ring[:, slot, (k % 2) * PIECE:(k % 2 + 1) * PIECE]
                if k % 2 == 0:
                    dve.wait_ge(unit_loaded[slot], piece * 16 + 16)
                if tiles_before is None or tiles_before + k >= 2:
                    dve.wait_ge(tile_used, n - 1)
                V.tensor_copy(w_hi[:, k % 2, :], raw).then_inc(hi_split, 1)
                dve.wait_ge(hi_split, n + 1)
                V.tensor_tensor(w_lo[:, k % 2, :], raw, w_hi[:, k % 2, :].bitcast(f32), ALU.subtract)\
                 .then_inc(tile_split, 1)

            dve.wait_ge(vecs_ready, 1)
            for g in range(KD // 2):
                b = 4 + g % 4
                dve.wait_ge(x_transposed, g + 1)
                if g >= 2:
                    dve.wait_ge(act_ready, g - 1)
                gain = vec_cols[:, 2 * g:2 * g + 2].unsqueeze(2).to_broadcast([P, 2, SEQ])
                V.tensor_tensor(xg_t[:, g % 2, :, :], bank[b][:, :].rearrange("p (k n) -> p k n", k=2), gain,
                                ALU.mult).then_inc(x_scaled, 1)
                if g >= 1:
                    split_tile(0, 2 * g - 2, tiles_before=0)
                dve.wait_ge(act_hi_ready, g + 1)
                V.tensor_tensor(act_lo[:, 2 * g:2 * g + 2, :], xg_t[:, g % 2, :, :],
                                act_hi[:, 2 * g:2 * g + 2, :].bitcast(f32), ALU.subtract).then_inc(act_ready, 1)
                if g >= 1:
                    split_tile(0, 2 * g - 1, tiles_before=0)
            split_tile(0, KD - 2)
            split_tile(0, KD - 1)
            dve.wait_ge(roots_done, 1)
            V.reciprocal(rinv[:, 0:2], root[:, 0:2]).then_inc(rinv_ready, 1)
            with dve.Fori(1, PIECES_IN - 1) as piece:
                for k in range(KD):
                    split_tile(piece, k)

            def scale_v(b):
                V.scalar_tensor_tensor(out=v[:, b, :], in0=v[:, b, :], scalar=rinv[:, 2 + b:3 + b],
                                       in1=gain_bc[:, :], op0=ALU.mult, op1=ALU.mult).then_inc(v_ready, 1)

            def gate_head(h):
                dve.wait_ge(mixed, h + 1)
                for b in range(NB):
                    cols = slice(h * HD, (h + 1) * HD)
                    last = V.scalar_tensor_tensor(out=u[:, b, cols], in0=bank[h % 4][:, b * HD:(b + 1) * HD],
                                                  scalar=vec_cols[:, 2 * KD + h:2 * KD + h + 1],
                                                  in1=u[:, b, cols], op0=ALU.add, op1=ALU.mult)
                last.then_inc(gated, 1)

            def low_half(h):
                dve.wait_ge(act_hi_ready, KD // 2 + h + 1)
                V.tensor_tensor(act_lo[:, 2 * h:2 * h + 2, :].rearrange("p k n -> p (k n)"), bank[h % 4][:, :],
                                act_hi[:, 2 * h:2 * h + 2, :].rearrange("p k n -> p (k n)").bitcast(f32),
                                ALU.subtract).then_inc(act_ready, 1)

            def add_residual(piece):
                c0 = (piece - PIECES_IN) * PIECE
                dve.wait_ge(tile_used, KD * (piece + 1))
                for c in range(2):
                    for b in range(NB):
                        cols = slice(c0 + c * BANK, c0 + (c + 1) * BANK)
                        V.tensor_tensor(x[:, b, cols], x[:, b, cols],
                                        bank[4 * SET_OF[piece] + 2 * c + b][:, :], ALU.add).then_inc(h2_ready, 1)

            dve.wait_ge(roots_done, 2)
            V.reciprocal(rinv[:, 2:4], root[:, 2:4]).then_inc(rinv_ready, 1)
            dve.wait_ge(rinv_ready, 2)
            dve.wait_ge(gain_loaded, 16)
            for k in range(KD):
                split_tile(PIECES_IN - 1, k)
                if k in (2, 5):
                    scale_v(k // 3)
                if 8 <= k < 12:
                    if k == 8:
                        dve.wait_ge(z_ready, 12)
                    gate_head(k - 8)
                if k >= 13:
                    low_half(k - 13)
            split_tile(PIECES_IN, 0)
            low_half(3)
            split_tile(PIECES_IN, 1)
            dve.wait_ge(z_ready, 16)
            for h in range(4, HEADS):
                gate_head(h)
            for k in range(2, KD):
                split_tile(PIECES_IN, k)
                if 3 <= k < 7:
                    low_half(k + 1)
            split_tile(PIECES_IN + 1, 0)
            split_tile(PIECES_IN + 1, 1)
            add_residual(PIECES_IN)
            dve.wait_ge(consts_ready, 1)
            dve.wait_ge(router_loaded, 32)
            V.tensor_tensor(rwg[:, :, 0:E], rw[:, :, :],
                            vec_cols[:, KD:2 * KD].unsqueeze(2).to_broadcast([P, KD, E]), ALU.mult)\
             .then_inc(rwg_ready, 1)
            V.tensor_reduce(fold[:, :], ident[:, :].rearrange("p (q e) -> p e q", q=4)[:, 0:E, :], AX.X, ALU.add)\
             .then_inc(rwg_ready, 1)
            for k in range(2, KD):
                split_tile(PIECES_IN + 1, k)
            add_residual(PIECES_IN + 1)

            dve.wait_ge(h2_ready, 8)
            dve.wait_ge(sq_done, 3 * NB)
            for b in range(NB):
                V.tensor_tensor_reduce(out=acc[:, b, PIECE:D], in0=x[:, b, PIECE:D], in1=x[:, b, PIECE:D],
                                       scale=1.0, scalar=ss[:, 4 + b:5 + b], op0=ALU.mult, op1=ALU.add,
                                       accum_out=ss[:, 6 + b:7 + b]).then_inc(sq_v_done, 1)
            dve.wait_ge(roots_done, 3)
            V.reciprocal(rinv[:, 4:6], root[:, 4:6]).then_inc(rinv_ready, 1)
            dve.wait_ge(rinv_ready, 3)
            dve.wait_ge(consts_ready, 8)

            dve.wait_ge(logits_done, 1)
            link(V.tensor_reduce(red[:, :, 0:1], bank[1][:, 0:NB * E].rearrange("p (b e) -> p b e", b=NB), AX.X,
                                 ALU.max))
            V.scalar_tensor_tensor(out=red[:, :, 1], in0=red[:, :, 0], scalar=-1.0, in1=rinv[:, 4:6],
                                   op0=ALU.mult, op1=ALU.mult).then_inc(shift_ready, 1)
            dve.wait_ge(exp_done, NB)
            link(V.reciprocal(red[:, :, 3:4], red[:, :, 2:3]))
            for b in range(NB):
                V.scalar_tensor_tensor(out=sel[:, b * GROUPS:(b + 1) * GROUPS, :].rearrange("p g k -> p (g k)"),
                                       in0=expd[:, b, :], scalar=red[:, b, 3:4], in1=rb[:, 0, :],
                                       op0=ALU.mult, op1=ALU.add).then_inc(chain, 1)
            links[0] += NB
            dve.wait_ge(chain, links[0])

            four = [P, NB * GROUPS, PER_GROUP, PER_GROUP]
            link(V.tensor_tensor(diff[:, :, :, :], sel[:, :, :].unsqueeze(2).to_broadcast(four),
                                 sel[:, :, :].unsqueeze(3).to_broadcast(four), ALU.subtract))
            link(V.tensor_tensor(diff[:, :, :, :], diff[:, :, :, :], wins_from[:, :, :, :].to_broadcast(four),
                                 ALU.is_gt))
            link(V.tensor_reduce(beaten[:, :, :], diff[:, :, :, :], AX.X, ALU.add))
            link(V.scalar_tensor_tensor(out=top_sel[:, :, :], in0=beaten[:, :, :], scalar=1.5, in1=sel[:, :, :],
                                        op0=ALU.is_lt, op1=ALU.mult))
            link(V.tensor_reduce(gscore[:, :, :].rearrange("p b g -> p (b g)"), top_sel[:, :, :], AX.X, ALU.add))
            groups = [P, NB, GROUPS, GROUPS]
            link(V.tensor_tensor(gdiff[:, :, :, :], gscore[:, :, :].unsqueeze(2).to_broadcast(groups),
                                 gscore[:, :, :].unsqueeze(3).to_broadcast(groups), ALU.subtract))
            link(V.tensor_tensor(gdiff[:, :, :, :], gdiff[:, :, :, :], wins_from[:, :, :, :].to_broadcast(groups),
                                 ALU.is_gt))
            link(V.tensor_reduce(gbeaten[:, :, 0], gdiff[:, :, :, :].rearrange("p b k j -> p (b k) j"), AX.X, ALU.add))
            link(V.tensor_scalar(gpick[:, :, :], gbeaten[:, :, :], 0.5, None, ALU.is_lt))
            V.scalar_tensor_tensor(out=assigned[:, :, :].rearrange("p b (g k) -> p (b g) k", g=GROUPS),
                                   in0=beaten[:, :, :], scalar=1.5,
                                   in1=gpick[:, :, :].to_broadcast([P, NB * GROUPS, PER_GROUP]),
                                   op0=ALU.is_lt, op1=ALU.mult).then_inc(assigned_ready, 1)
            dve.wait_ge(assigned_ready, 1)
            link(V.tensor_tensor(wsel[:, :, :], expd[:, :, :], assigned[:, :, :], ALU.mult))
            link(V.tensor_reduce(red[:, :, 4:5], wsel[:, :, :], AX.X, ALU.add))
            link(V.reciprocal(red[:, :, 5:6], red[:, :, 4:5]))
            link(V.tensor_tensor(weight_of[:, :, 0:E], wsel[:, :, :], red[:, :, 5:6].to_broadcast([P, NB, E]), ALU.mult))
            dve.wait_ge(ranks_done, 1)
            link(V.scalar_tensor_tensor(out=rank_t[:, :, :], in0=bank[2][:, 0:NB * E].rearrange("p (b e) -> p b e", b=NB),
                                        scalar=FAR, in1=assigned[:, :, :], op0=ALU.add, op1=ALU.mult))
            link(V.tensor_scalar(rank_of[:, :, 0:E], rank_t[:, :, :], -FAR, None, ALU.add))
            for b in range(NB):
                last = V.tensor_scalar(pick[:, b, :], tok_of[:, 0:TOK], rank_of[:, b, 0:1], rinv[:, 4 + b:5 + b],
                                       ALU.is_equal, ALU.mult)
            last.then_inc(pick_ready, 1)

            def take_rows(n):
                dve.wait_ge(gathered, n)
                V.tensor_copy(x_row[:, 1, :], bank[7][:, :]).then_inc(row_b_ready, 1)

            def take_gathered(n):
                dve.wait_ge(row_transposed, n)
                for g in range(2):
                    dst = xg[:, 8 * g:8 * g + 8, :].rearrange("p (h s) t -> p s h t", h=2)
                    gain = vec_cols[:, KD + 8 * g:KD + 8 * g + 8].rearrange("p (h s) -> p s h", h=2)
                    last = V.tensor_tensor(dst, bank[6 + g][:, :].rearrange("p (s h t) -> p s h t", s=4, h=2),
                                           gain.unsqueeze(3).to_broadcast([P, 4, 2, TOK]), ALU.mult)
                last.then_inc(xg_ready, 1)

            count = bank[3][:, 0:E]
            link(V.tensor_scalar(extra[:, 0, :], count, TOK + 0.5, None, ALU.is_gt))
            for n in range(2, SEQ // TOK):
                link(V.scalar_tensor_tensor(out=extra[:, 0, :], in0=count, scalar=n * TOK + 0.5,
                                            in1=extra[:, 0, :], op0=ALU.is_gt, op1=ALU.add))
            link(V.tensor_tensor_scan(upto[:, 0, :], ones_row[:, :], extra[:, 0, :], 0.0, ALU.mult, ALU.add))
            V.tensor_scalar(last_index[:, :], upto[:, 0, E - 1:E], E - 1.0, None, ALU.add).then_inc(count_ready, 1)
            take_rows(1)
            take_gathered(1)
            link(V.tensor_tensor(start[:, 0, :], upto[:, 0, :], extra[:, 0, :], ALU.subtract))
            over = [P, MORE, E]
            q_wide = q_idx[:, :, :].to_broadcast(over)
            link(V.tensor_tensor(qa[:, :, :], upto[:, :, :].to_broadcast(over), q_wide, ALU.is_gt))
            link(V.tensor_tensor(qsel[:, :, :], start[:, :, :].to_broadcast(over), q_wide, ALU.is_le))
            link(V.tensor_tensor(qsel[:, :, :], qsel[:, :, :], qa[:, :, :], ALU.mult))
            link(V.tensor_tensor(qoff[:, :, :], start[:, :, :].to_broadcast(over), q_wide, ALU.subtract))
            link(V.tensor_scalar(qoff[:, :, :], qoff[:, :, :], -float(TOK), float(TOK), ALU.mult, ALU.add))
            for b in range(NB):
                link(V.tensor_tensor(qt[:, :, :], rank_of[:, b:b + 1, 0:E].to_broadcast(over), qoff[:, :, :],
                                     ALU.subtract))
                link(V.tensor_tensor(qt[:, :, :], qt[:, :, :], qsel[:, :, :], ALU.mult))
                link(V.tensor_reduce(rank_of[:, b, E:MAX_ITEMS], qt[:, :, :], AX.X, ALU.add))
                link(V.tensor_tensor(qt[:, :, :], weight_of[:, b:b + 1, 0:E].to_broadcast(over), qsel[:, :, :],
                                     ALU.mult))
                link(V.tensor_reduce(weight_of[:, b, E:MAX_ITEMS], qt[:, :, :], AX.X, ALU.add))
            link(V.tensor_tensor(qt[:, :, :], e_idx[:, :, :].to_broadcast(over), qsel[:, :, :], ALU.mult))
            link(V.tensor_reduce(ids_f[:, E:MAX_ITEMS], qt[:, :, :], AX.X, ALU.add))
            link(V.tensor_copy(ids_f[:, 0:E], e_idx[:, 0, :]))
            V.tensor_copy(item_expert[:, :], ids_f[:, :]).then_inc(tables_ready, 1)

            def add_back(scattered_before):
                for j in range(8):
                    b, c = j // 4, j % 4
                    dve.wait_ge(scattered, scattered_before + (j + 1))
                    cols = slice(c * BANK, (c + 1) * BANK)
                    V.tensor_tensor(acc[:, b, cols], acc[:, b, cols], bank[5 + j % 3][:, :], ALU.add)\
                     .then_inc(acc_added, 1)

            dve.wait_ge(tables_ready, 1)
            last_item = dve.value_load(last_index[0:1, 0:1], min_val=E - 1, max_val=MAX_ITEMS - 1)
            dve.wait_ge(acc_set, NB)

            def item(i, last=False):
                for b in range(NB):
                    ins = V.tensor_scalar(place[:, b, :], tok_of[:, :], rank_of[:, b, bass.ds(i, 1)],
                                          weight_of[:, b, bass.ds(i, 1)], ALU.is_equal, ALU.mult)
                ins.then_inc(place_ready, 1)
                if not last:
                    for b in range(NB):
                        ins = V.tensor_scalar(pick[:, b, :], tok_of[:, 0:TOK], rank_of[:, b, bass.ds(i + 1, 1)],
                                              rinv[:, 4 + b:5 + b], ALU.is_equal, ALU.mult)
                    ins.then_inc(pick_ready, 1)
                dve.wait_ge(sil_ready, i * 2 + 1)
                V.tensor_tensor(hid[TOK:P, :], sil[TOK:P, :], bank[0][TOK:P, :], ALU.mult)
                dve.wait_ge(sil_ready, i * 2 + 2)
                V.tensor_tensor(hid[0:TOK, :], sil[0:TOK, :], bank[1][0:TOK, :], ALU.mult).then_inc(hid_ready, 1)
                add_back(i * 8)
                if last:
                    dve.wait_ge(step_done, i * STEPS + STEPS)
                    V.tensor_copy(y[:, 1, :], bank[3][:, :]).then_inc(last_y_ready, 1)
                else:
                    take_rows(i + 2)
                    take_gathered(i + 2)

            with dve.Fori(0, last_item) as i:
                item(i)
            item(last_item, last=True)
            add_back(last_item * 8 + 8)

            dve.wait_ge(acc_added, last_item * 8 + 16)
            dve.wait_ge(sq_done, 3 * NB + 2)
            V.tensor_tensor_reduce(out=x[:, 1, PIECE:D], in0=acc[:, 1, PIECE:D], in1=acc[:, 1, PIECE:D], scale=1.0,
                                   scalar=ss[:, 5:6], op0=ALU.mult, op1=ALU.add, accum_out=ss[:, 6:7])\
             .then_inc(sq_v_done, 1)
            dve.wait_ge(gain_loaded, 32)
            for b in range(NB):
                dve.wait_ge(roots_done, 4 + b)
                V.reciprocal(rinv[:, b:b + 1], root[:, 4 + b:5 + b]).then_inc(rinv_ready, 1)
                dve.wait_ge(rinv_ready, 4 + b)
                for c in range(2):
                    cols = slice(c * PIECE, (c + 1) * PIECE)
                    V.scalar_tensor_tensor(out=acc[:, b, cols], in0=acc[:, b, cols], scalar=rinv[:, b:b + 1],
                                           in1=gain_bc[:, cols], op0=ALU.mult, op1=ALU.mult).then_inc(out_ready, 1)

        @block.tensor
        def _(pe):
            T = nc.tensor
            pe.wait_ge(ident_ready, 1)
            pe.wait_ge(vecs_loaded, 48)
            rows = 2 * KD + HEADS
            T.transpose(bank[0][:, 0:rows], vec_raw, ident[0:rows, 0:rows]).then_inc(vecs_transposed, 1)

            def transpose_pair(dst, src, g):
                for s in range(2):
                    for b in range(NB):
                        k = 2 * g + s
                        last = T.transpose(dst[:, s * SEQ + b * P:s * SEQ + (b + 1) * P],
                                           src[:, b, k * P:(k + 1) * P], ident[:, :])
                return last

            for g in range(4):
                if g % 2 == 0:
                    pe.wait_ge(x_loaded[g // 2], 16)
                transpose_pair(bank[4 + g], x, g).then_inc(x_transposed, 1)

            def project_slab(bank_set, k):
                last = None
                for c in range(2):
                    for b in range(NB):
                        dst = bank[4 * bank_set + 2 * c + b][:, :]
                        hi, lo = (t[:, k, b * P:(b + 1) * P] for t in (act_hi, act_lo))
                        wh, wl = (t[:, k % 2, c * BANK:(c + 1) * BANK] for t in (w_hi, w_lo))
                        T.matmul(dst, hi, wh, start=(k == 0), stop=False)
                        T.matmul(dst, hi, wl, start=False, stop=False)
                        last = T.matmul(dst, lo, wh, start=False, stop=(k == KD - 1))
                last.then_inc(tile_used, 1)

            pe.wait_ge(vecs_ready, 1)
            for k in range(KD):
                if k % 2 == 0 and 2 <= k < 10:
                    g = k // 2 + 3
                    if g % 2 == 0:
                        pe.wait_ge(x_loaded[g // 2], 16)
                    pe.wait_ge(x_scaled, g - 3)
                    transpose_pair(bank[4 + g % 4], x, g).then_inc(x_transposed, 1)
                if k == 12:
                    pe.wait_ge(ws_masked, 1)
                    for g in range(2):
                        pe.wait_ge(x_scaled, 5 + g)
                        for h in range(4):
                            last = T.transpose(bank[4 + g][:, h * P:(h + 1) * P], ws_raw[:, 4 * g + h, :],
                                               ident[:, :])
                        last.then_inc(ws_transposed, 1)
                if k % 2 == 0:
                    pe.wait_ge(act_ready, k // 2 + 1)
                pe.wait_ge(tile_split, k + 1)
                project_slab(0, k)
            pe.wait_ge(x_scaled, KD // 2)
            pe.wait_ge(ws_ready, 2)
            for k in range(KD):
                pe.wait_ge(tile_split, KD + k + 1)
                project_slab(1, k)
            pe.wait_ge(z_ready, 4)
            for k in range(KD):
                pe.wait_ge(tile_split, 2 * KD + k + 1)
                project_slab(0, k)

            def mix_heads(heads):
                for h in heads:
                    for b in range(NB):
                        last = T.matmul(bank[h % 4][:, b * HD:(b + 1) * HD], ws_t[:, h, :],
                                        v[:, b, h * HD:(h + 1) * HD], start=True, stop=True)
                    last.then_inc(mixed, 1)

            pe.wait_ge(z_ready, 8)
            for k in range(KD):
                if k == 8:
                    pe.wait_ge(v_ready, NB)
                    pe.wait_ge(z_ready, 12)
                    mix_heads(range(4))
                if k >= 12:
                    pe.wait_ge(gated, k - 11)
                    transpose_pair(bank[k - 12], u, k - 12).then_inc(gated_t, 1)
                pe.wait_ge(tile_split, 3 * KD + k + 1)
                project_slab(1, k)
            pe.wait_ge(act_ready, KD // 2 + 4)
            mix_heads(range(4, HEADS))

            pe.wait_ge(z_ready, 16)
            for k in range(KD):
                if 2 <= k < 6:
                    pe.wait_ge(gated, k + 3)
                    transpose_pair(bank[k - 2], u, k + 2).then_inc(gated_t, 1)
                if k >= 8 and k % 2 == 0:
                    pe.wait_ge(act_ready, KD // 2 + k // 2 + 1)
                pe.wait_ge(tile_split, 4 * KD + k + 1)
                project_slab(SET_OF[PIECES_IN], k)
            for k in range(KD):
                pe.wait_ge(tile_split, 5 * KD + k + 1)
                project_slab(SET_OF[PIECES_IN + 1], k)
                if k == 7:
                    pe.wait_ge(h2_ready, 4)
                    for g in range(4):
                        transpose_pair(bank[4 + g], x, g).then_inc(h2_transposed, 1)
            pe.wait_ge(h2_t_ready, 4)
            for g in range(4):
                if g % 2 == 0:
                    pe.wait_ge(h2_ready, 6 + g)
                transpose_pair(bank[4 + g], x, 4 + g).then_inc(h2_transposed, 1)

            pe.wait_ge(h2_ready, 8)
            pe.wait_ge(rwg_ready, 1)
            for k in range(KD):
                if k >= 8 and k % 2 == 0:
                    pe.wait_ge(h2_t_ready, k // 2 + 1)
                q = k % 4
                last = T.matmul(bank[0][q * QUAD:(q + 1) * QUAD, 0:SEQ], rwg[:, k, :], h2_t[:, k, :],
                                start=(k < 4), stop=(k >= KD - 4), tile_position=(0, q * QUAD))
            last.then_inc(quarters_done, 1)
            pe.wait_ge(quarter_ready, 1)
            pe.wait_ge(rwg_ready, 2)
            for b in range(NB):
                last = T.matmul(bank[1][:, b * E:(b + 1) * E], quarter[:, b * P:(b + 1) * P], fold[:, :],
                                start=True, stop=True)
            last.then_inc(logits_done, 1)
            pe.wait_ge(assigned_ready, 1)
            flat = assigned[:, :, :].rearrange("p b e -> p (b e)")
            T.matmul(bank[2][:, 0:NB * E], before[:, :], flat, start=True, stop=False)
            T.matmul(bank[2][:, E:2 * E], ones[:, :], assigned[:, 0, :], start=False, stop=True)
            for b in range(NB):
                last = T.matmul(bank[3][:, 0:E], ones[:, :], assigned[:, b, :], start=(b == 0), stop=(b == NB - 1))
            last.then_inc(ranks_done, 1)

            def gather():
                for jj in range(2):
                    for b in range(NB):
                        for h in range(2):
                            c = 2 * jj + h
                            last = T.matmul(bank[6 + jj][h * TOK:(h + 1) * TOK, :], pick[:, b, :],
                                            x[:, b, c * BANK:(c + 1) * BANK], start=(b == 0), stop=(b == NB - 1))
                last.then_inc(gathered, 1)

            def transpose_rows(n):
                pe.wait_ge(row_a_ready, n)
                pe.wait_ge(row_b_ready, n)
                for jj in range(2):
                    for g in range(4):
                        last = T.transpose(bank[6 + jj][:, g * P:(g + 1) * P], x_row[:, jj, g * P:(g + 1) * P],
                                           ident[:, :])
                last.then_inc(row_transposed, 1)

            def scatter(added_before, last=False):
                for j in range(8):
                    b, jj, h = j // 4, j % 4 // 2, j % 2
                    if last and j == 2:
                        pe.wait_ge(last_y_ready, 1)
                    if j >= 3:
                        pe.wait_ge(acc_added, added_before + (j - 2))
                    T.matmul(bank[5 + j % 3][:, :], back[h * TOK:(h + 1) * TOK, b * P:(b + 1) * P],
                             y[h * TOK:(h + 1) * TOK, jj, :], start=True, stop=True).then_inc(scattered, 1)

            pe.wait_ge(pick_ready, 1)
            gather()
            transpose_rows(1)
            pe.wait_ge(count_ready, 1)
            last_item = pe.value_load(last_index[0:1, 0:1], min_val=E - 1, max_val=MAX_ITEMS - 1)

            def item(i, last=False):
                pe.wait_ge(xg_ready, i + 1)
                for m in range(PIECE_UNITS):
                    for unit in (2 * m, 2 * m + 1):
                        pe.wait_ge(unit_loaded[slot_of(unit)], unit_count(i, unit))
                    for s in range(2):
                        for c in range(2):
                            for up in range(2):
                                at = TOK * ((up + c) % 2)
                                ins = T.matmul(bank[c][at:at + TOK, :], xg[:, 2 * m + s, :],
                                                slot(slot_of(2 * m + up))[:, s * F + c * BANK:s * F + (c + 1) * BANK],
                                                start=(m == 0 and s == 0), stop=(m == PIECE_UNITS - 1 and s == 1))
                    ins.then_inc(step_done, 1)
                pe.wait_ge(y_ready, i + 1)
                pe.wait_ge(back_ready, i + 1)
                scatter(i * 8)
                pe.wait_ge(acc_added, i * 8 + 8)
                pe.wait_ge(place_ready, i + 1)
                for b in range(NB):
                    ins = T.transpose(bank[5][:, b * P:(b + 1) * P], place[:, b, :], ident[:, :])
                ins.then_inc(place_transposed, 1)
                if not last:
                    pe.wait_ge(pick_ready, i + 2)
                    gather()
                pe.wait_ge(hid_ready, i + 1)
                for f in range(4):
                    ins = T.transpose(bank[4][:, f * P:(f + 1) * P], hid[:, f * P:(f + 1) * P], ident[:, :])
                ins.then_inc(hid_transposed, 1)
                if not last:
                    transpose_rows(i + 2)
                pe.wait_ge(hid_t_ready, i + 1)
                for f in range(KF):
                    unit = 2 * PIECE_UNITS + f
                    pe.wait_ge(unit_loaded[slot_of(unit)], unit_count(i, unit))
                    hidden = hid_t[:, f % 4, TOK:P] if f < 4 else hid_t[:, f % 4, 0:TOK]
                    for c in range(4):
                        at = TOK * (c % 2)
                        ins = T.matmul(bank[2 + c // 2][at:at + TOK, :], hidden,
                                        slot(slot_of(unit))[:, c * BANK:(c + 1) * BANK],
                                        start=(f == 0), stop=(f == KF - 1))
                    ins.then_inc(step_done, 1)

            with pe.Fori(0, last_item) as i:
                item(i)
            item(last_item, last=True)
            pe.wait_ge(y_ready, last_item + 2)
            pe.wait_ge(back_ready, last_item + 2)
            scatter(last_item * 8 + 8, last=True)


_INS = ['x', 'norm_mix_g', 'norm_ffn_g', 'final_g', 'a_w_in', 'a_v_gain', 'a_w_s', 'a_b_s', 'a_w_out',
        'router_w', 'router_b', 'moe_w_gate', 'moe_w_up', 'moe_w_down']


def kernel(**inputs):
    import numpy as np
    import concourse.bacc as bacc
    from concourse.bass_utils import run_bass_kernel_spmd

    nc = bacc.Bacc("TRN2", target_bir_lowering=False, num_devices=1)
    arrays, args = {}, []
    for name in _INS:
        a = np.ascontiguousarray(inputs[name])
        arrays[f"in_{name}"] = a
        args.append(nc.dram_tensor(f"in_{name}", a.shape, mybir.dt.from_np(a.dtype), kind="ExternalInput").ap())
    shape = inputs['x'].shape
    args.append(nc.dram_tensor("out", shape, mybir.dt.float32, kind="ExternalOutput").ap())
    hybrid_trunk_kernel(nc, *args)
    r = run_bass_kernel_spmd(nc, [arrays], core_ids=[0])
    return r.results[0]["out"]
```

```python
import concourse.bass as bass
from concourse import mybir
from contextlib import ExitStack


def hybrid_trunk_kernel(nc, x_in, norm_mix_g, norm_ffn_g, final_g, a_w_in, a_v_gain, a_w_s, a_b_s,
                        a_w_out, router_w, router_b, w_gate, w_up, w_down, out):
    f32, f32r, bf16, i32 = mybir.dt.float32, mybir.dt.float32r, mybir.dt.bfloat16, mybir.dt.int32
    ALU = mybir.AluOpType
    ACT = mybir.ActivationFunctionType
    AX = mybir.AxisListType

    P = 128
    SEQ, D = x_in.shape[1], x_in.shape[2]
    NB = SEQ // P
    KD = D // P
    HEADS, CHUNK = a_w_s.shape[1], a_w_s.shape[2]
    HD = D // HEADS
    E, F = w_gate.shape[1], w_gate.shape[3]
    GROUPS = 4
    PER_GROUP = E // GROUPS
    TOK = 64
    BANK = 512
    PIECE = 1024
    RING = 13
    SLOTS = 19
    PIECE_UNITS = KD // 2
    PIECES_IN, PIECES_OUT = 2 * D // PIECE, D // PIECE
    PIECES = PIECES_IN + PIECES_OUT
    V_PARTS = (SEQ // P) * (D // BANK)
    REUSE = 12
    ITEM_UNITS = 24
    STEPS = 16
    KF = F // P
    MORE = 8
    MAX_ITEMS = E + MORE
    RMS_EPS = 1e-6
    BIG = 1e30
    TINY = 1.2e-38
    QUAD = 32
    SET_OF = [0, 1, 0, 1, 1, 0]
    FAR = 1024.0

    with ExitStack() as ctx:
        def sb(name, shape, dt=f32, at=ctx):
            return at.enter_context(nc.sbuf_tensor(name, shape, dt))

        def sem(name):
            return ctx.enter_context(nc.semaphore(name))

        ring = sb("ring", [P, RING, 2048])
        gain_bc = ring[:, RING - 1, :]
        x = sb("x", [P, NB, D])
        ident = sb("ident", [P, P])
        vec_cols = sb("vec_cols", [P, 2 * KD + HEADS])
        rw = sb("rw", [P, KD, E])
        rb = sb("rb", [P, 1, E])
        eps = sb("eps", [P, 2])
        ss = sb("ss", [P, 8])
        root = sb("root", [P, 8])
        rinv = sb("rinv", [P, 8])

        mix = ExitStack()
        z = sb("z", [P, 2, NB, D], at=mix)
        ws_t = sb("ws_t", [P, HEADS, CHUNK], at=mix)
        act_hi = sb("act_hi", [P, KD, SEQ], f32r, at=mix)
        act_lo = sb("act_lo", [P, KD, SEQ], f32r, at=mix)
        w_hi = sb("w_hi", [P, 2, PIECE], f32r, at=mix)
        w_lo = sb("w_lo", [P, 2, PIECE], f32r, at=mix)
        v, u = z[:, 0, :, :], z[:, 1, :, :]
        scratch = z[:, 1, :, :].rearrange("p n d -> p (n d)")
        ws_raw = scratch[:, 0:HEADS * CHUNK].rearrange("p (h s) -> p h s", h=HEADS)
        xg_t = scratch[:, 1024:2048].rearrange("p (b k n) -> p b k n", b=2, k=2)
        vec_raw = scratch[0:2 * KD + HEADS, 2048:2176]
        mix.close()

        routing = ExitStack()
        h2_t = sb("h2_t", [P, KD, SEQ], at=routing)
        routing.close()
        last_slot = sb("last_slot", [P, 2048])
        x_row = sb("x_row", [P, BANK])
        sil = sb("sil", [P, BANK])
        hid = sil
        hid_t = sil[:, :].rearrange("p (f t) -> p f t", f=4)
        quarter = sb("quarter", [P, SEQ])
        place = sb("place", [P, NB, 2 * TOK])
        qa = sb("qa", [P, MORE, E])
        qsel = sb("qsel", [P, MORE, E])
        qoff = sb("qoff", [P, MORE, E])
        qt = sb("qt", [P, MORE, E])
        acc = sb("acc", [P, NB, D])
        before = sb("before", [P, P], bf16)
        ones = sb("ones", [P, P], bf16)
        ones_row = sb("ones_row", [P, E])
        q_i = sb("q_i", [P, MORE], i32)
        q_idx = sb("q_idx", [P, MORE, 1])
        fold = sb("fold", [P, E])
        tok_of = sb("tok_of", [P, 2 * TOK])
        tok_i = sb("tok_i", [P, 2 * TOK], i32)
        e_idx = sb("e_idx", [P, 1, E])
        e_i = sb("e_i", [P, E], i32)
        later_i = sb("later_i", [P, PER_GROUP, PER_GROUP], i32)
        wins_from = sb("wins_from", [P, 1, PER_GROUP, PER_GROUP])
        y = sb("y", [P, 2, BANK])
        rwg = y[:, 0, :].rearrange("p (k e) -> p k e", k=KD)
        xg = sb("xg", [P, KD, TOK])
        back = sb("back", [P, SEQ])
        pick = sb("pick", [P, NB, TOK])
        expd = sb("expd", [P, NB, E])
        sel = sb("sel", [P, NB * GROUPS, PER_GROUP])
        red = sb("red", [P, NB, 8])
        diff = sb("diff", [P, NB * GROUPS, PER_GROUP, PER_GROUP])
        beaten = sb("beaten", [P, NB * GROUPS, PER_GROUP])
        top_sel = sb("top_sel", [P, NB * GROUPS, PER_GROUP])
        gscore = sb("gscore", [P, NB, GROUPS])
        gdiff = sb("gdiff", [P, NB, GROUPS, GROUPS])
        gbeaten = sb("gbeaten", [P, NB * GROUPS, 1])
        gpick = sb("gpick", [P, NB * GROUPS, 1])
        assigned = sb("assigned", [P, NB, E], bf16)
        wsel = sb("wsel", [P, NB, E])
        extra = sb("extra", [P, 1, E])
        upto = sb("upto", [P, 1, E])
        start = sb("start", [P, 1, E])
        rank_of = sb("rank_of", [P, NB, MAX_ITEMS + 2])
        weight_of = sb("weight_of", [P, NB, MAX_ITEMS + 2])
        more_slots = sb("more_slots", [P, SLOTS - 1 - RING, 2048])
        ids_f = sb("ids_f", [P, MAX_ITEMS])
        item_expert = sb("item_expert", [P, MAX_ITEMS], i32)
        last_index = sb("last_index", [P, 1], i32)

        bank = [ctx.enter_context(nc.psum_tensor(f"bank{b}", [P, BANK], f32)) for b in range(8)]

        x_loaded = [sem(f"x_loaded{b}") for b in range(4)]
        first_x_loaded = sem("first_x_loaded")
        first_slab_loaded = sem("first_slab_loaded")
        vecs_loaded = sem("vecs_loaded")
        ws_loaded = sem("ws_loaded")
        router_loaded = sem("router_loaded")
        gain_loaded = sem("gain_loaded")
        unit_loaded = [sem(f"unit_loaded{s}") for s in range(SLOTS)]
        ident_ready = sem("ident_ready")
        ws_masked = sem("ws_masked")
        vecs_transposed = sem("vecs_transposed")
        vecs_ready = sem("vecs_ready")
        x_transposed = sem("x_transposed")
        x_scaled = sem("x_scaled")
        act_hi_ready = sem("act_hi_ready")
        act_ready = sem("act_ready")
        ws_transposed = sem("ws_transposed")
        ws_ready = sem("ws_ready")
        hi_split = sem("hi_split")
        tile_split = sem("tile_split")
        tile_used = sem("tile_used")
        half_done = sem("half_done")
        sq_done = sem("sq_done")
        sq_v_done = sem("sq_v_done")
        roots_done = sem("roots_done")
        norm_chain = sem("norm_chain")
        rinv_ready = sem("rinv_ready")
        z_ready = sem("z_ready")
        v_ready = sem("v_ready")
        mixed = sem("mixed")
        gated = sem("gated")
        gated_t = sem("gated_t")
        h2_ready = sem("h2_ready")
        h2_transposed = sem("h2_transposed")
        h2_t_ready = sem("h2_t_ready")
        consts_ready = sem("consts_ready")
        pool_step = sem("pool_step")
        rwg_ready = sem("rwg_ready")
        logits_done = sem("logits_done")
        quarters_done = sem("quarters_done")
        quarter_ready = sem("quarter_ready")
        shift_ready = sem("shift_ready")
        exp_done = sem("exp_done")
        assigned_ready = sem("assigned_ready")
        ranks_done = sem("ranks_done")
        count_ready = sem("count_ready")
        tables_ready = sem("tables_ready")
        row_a_ready = sem("row_a_ready")
        row_b_ready = sem("row_b_ready")
        row_transposed = sem("row_transposed")
        chain = sem("chain")
        acc_set = sem("acc_set")
        pick_ready = sem("pick_ready")
        place_ready = sem("place_ready")
        gathered = sem("gathered")
        xg_ready = sem("xg_ready")
        step_done = sem("step_done")
        sil_ready = sem("sil_ready")
        hid_ready = sem("hid_ready")
        hid_transposed = sem("hid_transposed")
        hid_t_ready = sem("hid_t_ready")
        y_ready = sem("y_ready")
        last_y_half_done = sem("last_y_half_done")
        last_y_ready = sem("last_y_ready")
        place_transposed = sem("place_transposed")
        back_ready = sem("back_ready")
        scattered = sem("scattered")
        acc_added = sem("acc_added")
        out_ready = sem("out_ready")
        stored = sem("stored")

        w_in_v = a_w_in[0].rearrange("(k p) c -> p k c", p=P)
        w_out_v = a_w_out[0].rearrange("(k p) c -> p k c", p=P)
        gate_v = w_gate[0].rearrange("e (k p) c -> p e k c", p=P)
        up_v = w_up[0].rearrange("e (k p) c -> p e k c", p=P)
        down_v = w_down[0].rearrange("e (k p) c -> p e k c", p=P)
        x_v = x_in[0].rearrange("(b p) d -> p b d", p=P)
        out_v = out[0].rearrange("(b p) d -> p b d", p=P)

        def slot_of(unit):
            if unit >= SLOTS:
                unit -= REUSE
            return unit + PIECE_UNITS if unit < RING - PIECE_UNITS else unit - (RING - PIECE_UNITS) if unit < RING else unit

        def shared(unit):
            return SLOTS - REUSE <= unit < ITEM_UNITS - REUSE or unit >= SLOTS

        def slot(s):
            return ring[:, s, :] if s < RING else more_slots[:, s - RING, :] if s < SLOTS - 1 else last_slot[:, :]

        final_gain = slot(slot_of(0))

        def unit_count(i, unit):
            mixer = PIECES if slot_of(unit) < PIECE_UNITS else 0
            return i * (32 if shared(unit) else 16) + 16 * (mixer + (2 if unit >= SLOTS else 1))

        def step_of(unit):
            return unit // 2 if unit < 2 * PIECE_UNITS else unit - PIECE_UNITS

        block = ctx.enter_context(nc.Block())

        @block.sync
        def _(sp):
            sp.dma_start(vec_raw[0:KD, :], norm_mix_g[0].rearrange("(k p) -> k p", p=P)).then_inc(vecs_loaded, 16)
            sp.dma_start(vec_raw[KD:2 * KD, :], norm_ffn_g[0].rearrange("(k p) -> k p", p=P)).then_inc(vecs_loaded, 16)
            sp.dma_start(vec_raw[2 * KD:2 * KD + HEADS, :], a_b_s[0]).then_inc(vecs_loaded, 16)

            def load_x(c):
                cols = slice(c * BANK, (c + 1) * BANK)
                sp.dma_start(x[:, :, cols], x_v[:, :, cols]).then_inc(x_loaded[c], 16)

            first = 2 * P
            sp.dma_start(x[:, :, 0:first], x_v[:, :, 0:first]).then_inc(first_x_loaded, 16)
            sp.dma_start(ring[:, 0, 0:PIECE], w_in_v[:, 0, D:D + PIECE]).then_inc(first_slab_loaded, 16)
            sp.dma_start(x[:, :, first:BANK], x_v[:, :, first:BANK]).then_inc(x_loaded[0], 16)
            sp.dma_start(ring[:, 0, PIECE:2 * PIECE], w_in_v[:, 1, D:D + PIECE]).then_inc(unit_loaded[0], 16)
            load_x(1)
            for p in range(PIECES):
                for j in range(0 if p else 1, PIECE_UNITS):
                    if p >= 1:
                        sp.wait_ge(tile_split, KD * (p - 1) + 2 * j + 2)
                    if p < PIECES_IN:
                        c = ((p + 2) % PIECES_IN) * PIECE
                        src = w_in_v[:, 2 * j:2 * j + 2, c:c + PIECE]
                    else:
                        c = (p - PIECES_IN) * PIECE
                        src = w_out_v[:, 2 * j:2 * j + 2, c:c + PIECE]
                    sp.dma_start(ring[:, j, :].rearrange("p (k c) -> p k c", k=2), src)\
                      .then_inc(unit_loaded[j], 16)
                    if p == 0 and j < 3:
                        load_x(j + 1)

            def load_unit(expert, unit):
                dst = slot(slot_of(unit))
                if unit < 2 * PIECE_UNITS:
                    m, w = unit // 2, (gate_v, up_v)[unit % 2]
                    src = w[:, expert, 2 * m:2 * m + 2, :]
                    dst = dst.rearrange("p (k c) -> p k c", k=2)
                    if not isinstance(expert, int):
                        dst = dst.unsqueeze(1)
                else:
                    src = down_v[:, expert, unit - 2 * PIECE_UNITS, :]
                    if not isinstance(expert, int):
                        dst = dst.unsqueeze(1)
                sp.dma_start(dst, src).then_inc(unit_loaded[slot_of(unit)], 16)

            def load_next(i, expert, units):
                for unit in units:
                    if unit >= SLOTS:
                        sp.wait_ge(step_done, i * STEPS + (step_of(unit - REUSE) + 1))
                    elif shared(unit):
                        sp.wait_ge(step_done, i * STEPS + (step_of(unit + REUSE) + 1 - STEPS))
                    else:
                        sp.wait_ge(step_done, i * STEPS + (step_of(unit) + 1 - STEPS))
                    load_unit(expert, unit)

            for unit in range(SLOTS):
                if unit == SLOTS - 1:
                    sp.wait_ge(quarters_done, 1)
                elif unit >= RING:
                    sp.wait_ge(tile_used, KD * PIECES)
                elif unit >= RING - PIECE_UNITS:
                    sp.wait_ge(tile_split, KD * (PIECES - 1) + 2 * slot_of(unit) + 2)
                elif slot_of(unit) == RING - 1:
                    sp.wait_ge(v_ready, V_PARTS)
                load_unit(0, unit)
            load_next(1, 1, range(SLOTS - REUSE))
            load_next(0, 0, range(SLOTS, ITEM_UNITS))
            load_next(1, 1, range(ITEM_UNITS - REUSE, 2 * PIECE_UNITS))
            load_next(1, 1, range(SLOTS - REUSE, ITEM_UNITS - REUSE))
            load_next(1, 1, range(2 * PIECE_UNITS, SLOTS))
            load_next(2, 2, range(SLOTS - REUSE))
            load_next(1, 1, range(SLOTS, ITEM_UNITS))
            load_next(2, 2, range(SLOTS - REUSE, ITEM_UNITS))

            sp.wait_ge(tables_ready, 1)
            last_item = sp.value_load(last_index[0:1, 0:1], min_val=E - 1, max_val=MAX_ITEMS - 1)
            with sp.Fori(3, last_item + 1) as i:
                expert = bass.ds(sp.value_load(item_expert[0:1, bass.ds(i, 1)], min_val=0, max_val=E - 1), 1)
                load_next(i, expert, range(ITEM_UNITS))
            sp.dma_start(final_gain, final_g.rearrange("(a d) -> a d", a=1).to_broadcast([P, D]))\
              .then_inc(gain_loaded, 16)

            for n in range(2 * NB):
                b, c = n // 2, n % 2 * PIECE
                sp.wait_ge(out_ready, n + 1)
                sp.dma_start(out_v[:, b, c:c + PIECE], acc[:, b, c:c + PIECE]).then_inc(stored, 16)
            sp.wait_ge(stored, 16 * 2 * NB)

        @block.gpsimd
        def _(pool):
            nc.gpsimd.memset(ident[:, :], 0.0).then_inc(pool_step, 1)
            nc.gpsimd.memset(eps[:, :], RMS_EPS).then_inc(pool_step, 1)
            pool.wait_ge(pool_step, 2)
            nc.gpsimd.affine_select(out=ident[:, :], in_=ident[:, :], compare_op=ALU.not_equal, fill=1.0,
                                    base=0, pattern=[[-1, P]], channel_multiplier=1).then_inc(ident_ready, 1)
            pool.wait_ge(ws_loaded, 16)
            nc.gpsimd.affine_select(out=ws_raw, in_=ws_raw, compare_op=ALU.is_ge, fill=0.0, base=0,
                                    pattern=[[0, HEADS], [-1, CHUNK]], channel_multiplier=1).then_inc(ws_masked, 1)
            pool.wait_ge(mixed, HEADS)
            nc.gpsimd.memset(rwg[:, :, :], 0.0).then_inc(consts_ready, 1)
            nc.gpsimd.memset(ones[:, :], 1.0).then_inc(pool_step, 1)
            nc.gpsimd.memset(ones_row[:, :], 1.0).then_inc(pool_step, 1)
            nc.gpsimd.memset(before[:, :], 1.0).then_inc(pool_step, 1)
            nc.gpsimd.iota(tok_i[:, :], pattern=[[0, 2], [1, TOK]], base=0, channel_multiplier=0).then_inc(pool_step, 1)
            nc.gpsimd.iota(e_i[:, :], pattern=[[1, E]], base=0, channel_multiplier=0).then_inc(pool_step, 1)
            nc.gpsimd.iota(later_i[:, :, :], pattern=[[-1, PER_GROUP], [1, PER_GROUP]], base=0,
                           channel_multiplier=0).then_inc(pool_step, 1)
            nc.gpsimd.iota(q_i[:, :], pattern=[[1, MORE]], base=0, channel_multiplier=0).then_inc(pool_step, 1)
            pool.wait_ge(pool_step, 9)
            nc.gpsimd.affine_select(out=before[:, :], in_=before[:, :], compare_op=ALU.is_gt, fill=0.0, base=0,
                                    pattern=[[1, P]], channel_multiplier=-1).then_inc(pool_step, 1)
            pool.wait_ge(pool_step, 10)
            nc.gpsimd.affine_select(out=before[:, :], in_=before[:, :], compare_op=ALU.not_equal, fill=FAR, base=0,
                                    pattern=[[1, P]], channel_multiplier=-1).then_inc(consts_ready, 1)
            nc.gpsimd.tensor_copy(tok_of[:, :], tok_i[:, :]).then_inc(consts_ready, 1)
            nc.gpsimd.tensor_copy(e_idx[:, 0, :], e_i[:, :]).then_inc(consts_ready, 1)
            nc.gpsimd.tensor_scalar(wins_from[:, 0, :, :], later_i[:, :, :], 0.0, -TINY, ALU.is_lt, ALU.mult)\
              .then_inc(consts_ready, 1)
            nc.gpsimd.tensor_copy(q_idx[:, :, 0], q_i[:, :]).then_inc(consts_ready, 1)
            pool.wait_ge(tile_used, KD * PIECES)
            nc.gpsimd.memset(rank_of[:, :, :], -FAR).then_inc(consts_ready, 1)
            nc.gpsimd.memset(weight_of[:, :, :], 0.0).then_inc(consts_ready, 1)
            nc.gpsimd.memset(back[:, :], 0.0).then_inc(back_ready, 1)
            pool.wait_ge(quarters_done, 1)
            nc.gpsimd.memset(y[:, :, :], 0.0).then_inc(y_ready, 1)

        @block.scalar
        def _(act):
            act.wait_ge(vecs_transposed, 1)
            nc.scalar.copy(vec_cols[:, :], bank[0][:, 0:2 * KD + HEADS]).then_inc(vecs_ready, 1)
            for g in range(KD // 2):
                act.wait_ge(x_scaled, g + 1)
                nc.scalar.copy(act_hi[:, 2 * g:2 * g + 2, :], xg_t[:, g % 2, :, :]).then_inc(act_hi_ready, 1)
                if g == 2:
                    act.dma_start(ws_raw, a_w_s[0].rearrange("h t s -> t h s")).then_inc(ws_loaded, 16)
                    act.dma_start(gain_bc[:, :], a_v_gain.to_broadcast([P, D])).then_inc(gain_loaded, 16)
                    act.dma_start(rw[:, :, :], router_w.rearrange("(k p) e -> p k e", p=P)).then_inc(router_loaded, 16)
                    act.dma_start(rb[:, 0, :], router_b.rearrange("(a e) -> a e", a=1).to_broadcast([P, E]))\
                       .then_inc(router_loaded, 16)
            for g in range(2):
                act.wait_ge(ws_transposed, g + 1)
                nc.scalar.copy(ws_t[:, 4 * g:4 * g + 4, :].rearrange("p h s -> p (h s)"), bank[4 + g][:, :])\
                  .then_inc(ws_ready, 1)
            act.wait_ge(first_x_loaded, 16)
            for c in range(4):
                act.wait_ge(x_loaded[c], 16)
            for b in range(NB):
                nc.scalar.activation(v[:, b, :], x[:, b, :], ACT.Square, accum_out=ss[:, b:b + 1]).then_inc(sq_done, 1)
            act.wait_ge(sq_done, NB)
            nc.scalar.activation(root[:, 0:2], ss[:, 0:2], ACT.Sqrt, bias=eps[:, 0:1], scale=1.0 / D)\
              .then_inc(roots_done, 1)

            def gelu_piece(p):
                half, c0 = p // 2, p % 2 * PIECE
                act.wait_ge(tile_used, KD * (p + 1))
                for c in range(2):
                    for b in range(NB):
                        last = nc.scalar.activation(z[:, half, b, c0 + c * BANK:c0 + (c + 1) * BANK],
                                                    bank[4 * (p % 2) + 2 * c + b][:, :], ACT.Gelu_apprx_tanh,
                                                    scale=rinv[:, b:b + 1])
                        last.then_inc(z_ready, 1)

            act.wait_ge(rinv_ready, 1)
            gelu_piece(0)
            gelu_piece(1)
            act.wait_ge(z_ready, 8)
            for b in range(NB):
                nc.scalar.activation(u[:, b, :], v[:, b, :], ACT.Square, accum_out=ss[:, 2 + b:3 + b])\
                  .then_inc(sq_done, 1)
            act.wait_ge(sq_done, 2 * NB)
            nc.scalar.activation(root[:, 2:4], ss[:, 2:4], ACT.Sqrt, bias=eps[:, 0:1], scale=1.0 / D)\
              .then_inc(roots_done, 1)
            gelu_piece(2)

            def high_halves(heads):
                for h in heads:
                    act.wait_ge(gated_t, h + 1)
                    nc.scalar.copy(act_hi[:, 2 * h:2 * h + 2, :].rearrange("p k n -> p (k n)"), bank[h % 4][:, :])\
                      .then_inc(act_hi_ready, 1)

            high_halves(range(4))
            gelu_piece(3)
            high_halves(range(4, HEADS))

            def h2_by_features(half):
                for g in range(4 * half, 4 * half + 4):
                    act.wait_ge(h2_transposed, g + 1)
                    nc.scalar.copy(h2_t[:, 2 * g:2 * g + 2, :].rearrange("p k n -> p (k n)"), bank[4 + g % 4][:, :])\
                      .then_inc(h2_t_ready, 1)

            h2_by_features(0)
            for b in range(NB):
                nc.scalar.activation(acc[:, b, 0:PIECE], x[:, b, 0:PIECE], ACT.Square,
                                     accum_out=ss[:, 4 + b:5 + b]).then_inc(sq_done, 1)
            nc.scalar.activation(eps[:, 1:2], eps[:, 0:1], ACT.Sqrt)
            h2_by_features(1)
            act.wait_ge(sq_v_done, NB)
            nc.scalar.activation(root[:, 4:6], ss[:, 6:8], ACT.Sqrt, bias=eps[:, 0:1], scale=1.0 / D)\
              .then_inc(roots_done, 1)
            act.wait_ge(quarters_done, 1)
            nc.scalar.copy(quarter[:, :], bank[0][:, 0:SEQ]).then_inc(quarter_ready, 1)
            act.wait_ge(shift_ready, 1)
            for b in range(NB):
                nc.scalar.activation(expd[:, b, :], bank[1][:, b * E:(b + 1) * E], ACT.Exp, scale=rinv[:, 4 + b:5 + b],
                                     bias=red[:, b, 1:2], accum_out=red[:, b, 2:3]).then_inc(exp_done, 1)
            act.wait_ge(gathered, 1)
            nc.scalar.copy(x_row[:, :], bank[6][:, :]).then_inc(row_a_ready, 1)
            for b in range(NB):
                nc.scalar.copy(acc[:, b, :], x[:, b, :]).then_inc(acc_set, 1)

            act.wait_ge(count_ready, 1)
            last_item = act.value_load(last_index[0:1, 0:1], min_val=E - 1, max_val=MAX_ITEMS - 1)

            def item(i, last=False):
                act.wait_ge(place_transposed, i + 1)
                nc.scalar.copy(back[:, :], bank[5][:, 0:SEQ]).then_inc(back_ready, 1)
                if not last:
                    act.wait_ge(gathered, i * 2 + 3)
                    nc.scalar.copy(x_row[:, :], bank[6][:, :]).then_inc(row_a_ready, 1)
                act.wait_ge(step_done, i * STEPS + STEPS // 2)
                nc.scalar.activation(sil[TOK:P, :], bank[0][0:TOK, :], ACT.Silu).then_inc(sil_ready, 1)
                nc.scalar.activation(sil[0:TOK, :], bank[1][TOK:P, :], ACT.Silu).then_inc(sil_ready, 1)
                act.wait_ge(hid_transposed, i + 1)
                nc.scalar.copy(hid_t[:, :, :].rearrange("p f t -> p (f t)"), bank[4][:, :]).then_inc(hid_t_ready, 1)
                if last:
                    act.wait_ge(last_y_half_done, 1)
                    nc.scalar.copy(y[:, 0, :], bank[2][:, :]).then_inc(y_ready, 1)
                else:
                    act.wait_ge(step_done, i * STEPS + STEPS)
                    nc.scalar.copy(y[:, 0, :], bank[2][:, :])
                    nc.scalar.copy(y[:, 1, :], bank[3][:, :]).then_inc(y_ready, 1)

            with act.Fori(0, last_item) as i:
                item(i)
            item(last_item, last=True)

            nc.scalar.activation(eps[:, 1:2], eps[:, 0:1], ACT.Sqrt)
            links = 0
            for b, ends in ((0, (D - BANK, D)), (1, (PIECE, D - BANK, D))):
                bias, at = eps[:, 0:1], 0
                for part, end in enumerate(ends):
                    total, shifted = ss[:, 2 * b + part:2 * b + part + 1], root[:, 2 * b + part:2 * b + part + 1]
                    act.wait_ge(acc_added, last_item * 8 + (8 + 4 * b + end // BANK))
                    nc.scalar.activation(x[:, b, at:end], acc[:, b, at:end], ACT.Square, accum_out=total)\
                      .then_inc(norm_chain, 1)
                    links += 1
                    act.wait_ge(norm_chain, links)
                    if end < D:
                        nc.scalar.activation(shifted, total, ACT.Identity, bias=bias, scale=1.0 / D)\
                          .then_inc(norm_chain, 1)
                        links += 1
                        bias, at = shifted, end
                nc.scalar.activation(root[:, 4 + b:5 + b], total, ACT.Sqrt, bias=bias, scale=1.0 / D)\
                  .then_inc(roots_done, 1)

        @block.vector
        def _(dve):
            V = nc.vector
            links = [0]

            def link(ins):
                links[0] += 1
                ins.then_inc(chain, 1)
                dve.wait_ge(chain, links[0])

            def split_tile(piece, k, tiles_before=None):
                n = piece * KD + k
                slot = k // 2
                raw = ring[:, slot, (k % 2) * PIECE:(k % 2 + 1) * PIECE]
                if tiles_before is not None and k < 2:
                    dve.wait_ge((first_slab_loaded, unit_loaded[0])[k], 16)
                elif k % 2 == 0:
                    dve.wait_ge(unit_loaded[slot], piece * 16 + 16)
                if tiles_before is None or tiles_before + k >= 2:
                    dve.wait_ge(tile_used, n - 1)
                V.tensor_copy(w_hi[:, k % 2, :], raw).then_inc(hi_split, 1)
                dve.wait_ge(hi_split, n + 1)
                V.tensor_tensor(w_lo[:, k % 2, :], raw, w_hi[:, k % 2, :].bitcast(f32), ALU.subtract)\
                 .then_inc(tile_split, 1)

            dve.wait_ge(vecs_ready, 1)
            def scale_x(g):
                dve.wait_ge(x_transposed, g + 1)
                if g >= 2:
                    dve.wait_ge(act_ready, g - 1)
                gain = vec_cols[:, 2 * g:2 * g + 2].unsqueeze(2).to_broadcast([P, 2, SEQ])
                V.tensor_tensor(xg_t[:, g % 2, :, :], bank[4 + g % 4][:, :].rearrange("p (k n) -> p k n", k=2), gain,
                                ALU.mult).then_inc(x_scaled, 1)

            def low_half_of_x(g):
                dve.wait_ge(act_hi_ready, g + 1)
                V.tensor_tensor(act_lo[:, 2 * g:2 * g + 2, :], xg_t[:, g % 2, :, :],
                                act_hi[:, 2 * g:2 * g + 2, :].bitcast(f32), ALU.subtract).then_inc(act_ready, 1)

            scale_x(0)
            split_tile(0, 0, tiles_before=0)
            low_half_of_x(0)
            for g in range(1, KD // 2):
                scale_x(g)
                split_tile(0, 2 * g - 1, tiles_before=0)
                low_half_of_x(g)
                split_tile(0, 2 * g)
            split_tile(0, KD - 1)
            dve.wait_ge(roots_done, 1)
            V.reciprocal(rinv[:, 0:2], root[:, 0:2]).then_inc(rinv_ready, 1)
            with dve.Fori(1, PIECES_IN - 1) as piece:
                for k in range(KD):
                    split_tile(piece, k)

            def scale_v(part):
                b, cols = part % NB, slice(part // NB * BANK, (part // NB + 1) * BANK)
                V.scalar_tensor_tensor(out=v[:, b, cols], in0=v[:, b, cols], scalar=rinv[:, 2 + b:3 + b],
                                       in1=gain_bc[:, cols], op0=ALU.mult, op1=ALU.mult).then_inc(v_ready, 1)

            def gate_head(h):
                dve.wait_ge(mixed, h + 1)
                for b in range(NB):
                    cols = slice(h * HD, (h + 1) * HD)
                    last = V.scalar_tensor_tensor(out=u[:, b, cols], in0=bank[h % 4][:, b * HD:(b + 1) * HD],
                                                  scalar=vec_cols[:, 2 * KD + h:2 * KD + h + 1],
                                                  in1=u[:, b, cols], op0=ALU.add, op1=ALU.mult)
                last.then_inc(gated, 1)

            def low_half(h):
                dve.wait_ge(act_hi_ready, KD // 2 + h + 1)
                V.tensor_tensor(act_lo[:, 2 * h:2 * h + 2, :].rearrange("p k n -> p (k n)"), bank[h % 4][:, :],
                                act_hi[:, 2 * h:2 * h + 2, :].rearrange("p k n -> p (k n)").bitcast(f32),
                                ALU.subtract).then_inc(act_ready, 1)

            def add_residual(piece, c, blocks=range(NB)):
                for b in blocks:
                    at = (piece - PIECES_IN) * PIECE + c * BANK
                    V.tensor_tensor(x[:, b, at:at + BANK], x[:, b, at:at + BANK],
                                    bank[4 * SET_OF[piece] + 2 * c + b][:, :], ALU.add).then_inc(h2_ready, 1)

            dve.wait_ge(roots_done, 2)
            V.reciprocal(rinv[:, 2:4], root[:, 2:4]).then_inc(rinv_ready, 1)
            dve.wait_ge(rinv_ready, 2)
            dve.wait_ge(gain_loaded, 16)
            for k in range(KD):
                split_tile(PIECES_IN - 1, k)
                if k < V_PARTS:
                    scale_v(k)
                if 8 <= k < 12:
                    if k == 8:
                        dve.wait_ge(z_ready, 12)
                    gate_head(k - 8)
                if k >= 13:
                    low_half(k - 13)
            split_tile(PIECES_IN, 0)
            low_half(3)
            split_tile(PIECES_IN, 1)
            dve.wait_ge(z_ready, 16)
            for h in range(4, HEADS):
                gate_head(h)
            for k in range(2, KD):
                split_tile(PIECES_IN, k)
                if 3 <= k < 7:
                    low_half(k + 1)
            split_tile(PIECES_IN + 1, 0)
            split_tile(PIECES_IN + 1, 1)
            dve.wait_ge(tile_used, KD * (PIECES - 1))
            add_residual(PIECES_IN, 0)
            split_tile(PIECES_IN + 1, 2)
            add_residual(PIECES_IN, 1)
            split_tile(PIECES_IN + 1, 3)
            dve.wait_ge(consts_ready, 1)
            dve.wait_ge(router_loaded, 32)
            V.tensor_tensor(rwg[:, :, 0:E], rw[:, :, :],
                            vec_cols[:, KD:2 * KD].unsqueeze(2).to_broadcast([P, KD, E]), ALU.mult)\
             .then_inc(rwg_ready, 1)
            V.tensor_reduce(fold[:, :], ident[:, :].rearrange("p (q e) -> p e q", q=4)[:, 0:E, :], AX.X, ALU.add)\
             .then_inc(rwg_ready, 1)
            for k in range(4, KD):
                split_tile(PIECES_IN + 1, k)
            dve.wait_ge(half_done, 1)
            add_residual(PIECES_IN + 1, 0)
            dve.wait_ge(half_done, 2)
            add_residual(PIECES_IN + 1, 1, blocks=[0])
            dve.wait_ge(tile_used, KD * PIECES)
            add_residual(PIECES_IN + 1, 1, blocks=[1])
            dve.wait_ge(h2_ready, 8)
            dve.wait_ge(sq_done, 3 * NB)
            for b in range(NB):
                V.tensor_tensor_reduce(out=acc[:, b, PIECE:D], in0=x[:, b, PIECE:D], in1=x[:, b, PIECE:D],
                                       scale=1.0, scalar=ss[:, 4 + b:5 + b], op0=ALU.mult, op1=ALU.add,
                                       accum_out=ss[:, 6 + b:7 + b]).then_inc(sq_v_done, 1)
            dve.wait_ge(roots_done, 3)
            V.reciprocal(rinv[:, 4:6], root[:, 4:6]).then_inc(rinv_ready, 1)
            dve.wait_ge(rinv_ready, 3)
            dve.wait_ge(consts_ready, 8)

            dve.wait_ge(logits_done, 1)
            link(V.tensor_reduce(red[:, :, 0:1], bank[1][:, 0:NB * E].rearrange("p (b e) -> p b e", b=NB), AX.X,
                                 ALU.max))
            V.scalar_tensor_tensor(out=red[:, :, 1], in0=red[:, :, 0], scalar=-1.0, in1=rinv[:, 4:6],
                                   op0=ALU.mult, op1=ALU.mult).then_inc(shift_ready, 1)
            dve.wait_ge(exp_done, NB)
            link(V.reciprocal(red[:, :, 3:4], red[:, :, 2:3]))
            for b in range(NB):
                V.scalar_tensor_tensor(out=sel[:, b * GROUPS:(b + 1) * GROUPS, :].rearrange("p g k -> p (g k)"),
                                       in0=expd[:, b, :], scalar=red[:, b, 3:4], in1=rb[:, 0, :],
                                       op0=ALU.mult, op1=ALU.add).then_inc(chain, 1)
            links[0] += NB
            dve.wait_ge(chain, links[0])

            four = [P, NB * GROUPS, PER_GROUP, PER_GROUP]
            link(V.tensor_tensor(diff[:, :, :, :], sel[:, :, :].unsqueeze(2).to_broadcast(four),
                                 sel[:, :, :].unsqueeze(3).to_broadcast(four), ALU.subtract))
            link(V.tensor_tensor(diff[:, :, :, :], diff[:, :, :, :], wins_from[:, :, :, :].to_broadcast(four),
                                 ALU.is_gt))
            link(V.tensor_reduce(beaten[:, :, :], diff[:, :, :, :], AX.X, ALU.add))
            link(V.scalar_tensor_tensor(out=top_sel[:, :, :], in0=beaten[:, :, :], scalar=1.5, in1=sel[:, :, :],
                                        op0=ALU.is_lt, op1=ALU.mult))
            link(V.tensor_reduce(gscore[:, :, :].rearrange("p b g -> p (b g)"), top_sel[:, :, :], AX.X, ALU.add))
            groups = [P, NB, GROUPS, GROUPS]
            link(V.tensor_tensor(gdiff[:, :, :, :], gscore[:, :, :].unsqueeze(2).to_broadcast(groups),
                                 gscore[:, :, :].unsqueeze(3).to_broadcast(groups), ALU.subtract))
            link(V.tensor_tensor(gdiff[:, :, :, :], gdiff[:, :, :, :], wins_from[:, :, :, :].to_broadcast(groups),
                                 ALU.is_gt))
            link(V.tensor_reduce(gbeaten[:, :, 0], gdiff[:, :, :, :].rearrange("p b k j -> p (b k) j"), AX.X, ALU.add))
            link(V.tensor_scalar(gpick[:, :, :], gbeaten[:, :, :], 0.5, None, ALU.is_lt))
            V.scalar_tensor_tensor(out=assigned[:, :, :].rearrange("p b (g k) -> p (b g) k", g=GROUPS),
                                   in0=beaten[:, :, :], scalar=1.5,
                                   in1=gpick[:, :, :].to_broadcast([P, NB * GROUPS, PER_GROUP]),
                                   op0=ALU.is_lt, op1=ALU.mult).then_inc(assigned_ready, 1)
            dve.wait_ge(assigned_ready, 1)
            dve.wait_ge(ranks_done, 1)
            link(V.tensor_scalar(rank_of[:, :, 0:E], bank[2][:, 0:NB * E].rearrange("p (b e) -> p b e", b=NB),
                                 -FAR, None, ALU.add))
            for b in range(NB):
                last = V.tensor_scalar(pick[:, b, :], tok_of[:, 0:TOK], rank_of[:, b, 0:1], rinv[:, 4 + b:5 + b],
                                       ALU.is_equal, ALU.mult)
            last.then_inc(pick_ready, 1)

            def take_half(n, g):
                dve.wait_ge(row_transposed, 2 * n + (g + 1))
                dst = xg[:, 8 * g:8 * g + 8, :].rearrange("p (h s) t -> p s h t", h=2)
                gain = vec_cols[:, KD + 8 * g:KD + 8 * g + 8].rearrange("p (h s) -> p s h", h=2)
                V.tensor_tensor(dst, bank[6 + g][:, :].rearrange("p (s h t) -> p s h t", s=4, h=2),
                                gain.unsqueeze(3).to_broadcast([P, 4, 2, TOK]), ALU.mult).then_inc(xg_ready, 1)

            count = bank[3][:, 0:E]
            link(V.tensor_scalar(extra[:, 0, :], count, TOK + 0.5, None, ALU.is_gt))
            for n in range(2, SEQ // TOK):
                link(V.scalar_tensor_tensor(out=extra[:, 0, :], in0=count, scalar=n * TOK + 0.5,
                                            in1=extra[:, 0, :], op0=ALU.is_gt, op1=ALU.add))
            link(V.tensor_tensor_scan(upto[:, 0, :], ones_row[:, :], extra[:, 0, :], 0.0, ALU.mult, ALU.add))
            V.tensor_scalar(last_index[:, :], upto[:, 0, E - 1:E], E - 1.0, None, ALU.add).then_inc(count_ready, 1)
            link(V.tensor_tensor(wsel[:, :, :], expd[:, :, :], assigned[:, :, :], ALU.mult))
            link(V.tensor_reduce(red[:, :, 4:5], wsel[:, :, :], AX.X, ALU.add))
            link(V.reciprocal(red[:, :, 5:6], red[:, :, 4:5]))
            link(V.tensor_tensor(weight_of[:, :, 0:E], wsel[:, :, :], red[:, :, 5:6].to_broadcast([P, NB, E]),
                                 ALU.mult))
            take_half(0, 0)
            link(V.tensor_tensor(start[:, 0, :], upto[:, 0, :], extra[:, 0, :], ALU.subtract))
            over = [P, MORE, E]
            q_wide = q_idx[:, :, :].to_broadcast(over)
            link(V.tensor_tensor(qa[:, :, :], upto[:, :, :].to_broadcast(over), q_wide, ALU.is_gt))
            link(V.tensor_tensor(qsel[:, :, :], start[:, :, :].to_broadcast(over), q_wide, ALU.is_le))
            link(V.tensor_tensor(qsel[:, :, :], qsel[:, :, :], qa[:, :, :], ALU.mult))
            link(V.tensor_tensor(qoff[:, :, :], start[:, :, :].to_broadcast(over), q_wide, ALU.subtract))
            link(V.tensor_scalar(qoff[:, :, :], qoff[:, :, :], -float(TOK), float(TOK), ALU.mult, ALU.add))
            for b in range(NB):
                link(V.tensor_tensor(qt[:, :, :], rank_of[:, b:b + 1, 0:E].to_broadcast(over), qoff[:, :, :],
                                     ALU.subtract))
                link(V.tensor_tensor(qt[:, :, :], qt[:, :, :], qsel[:, :, :], ALU.mult))
                link(V.tensor_reduce(rank_of[:, b, E:MAX_ITEMS], qt[:, :, :], AX.X, ALU.add))
                link(V.tensor_tensor(qt[:, :, :], weight_of[:, b:b + 1, 0:E].to_broadcast(over), qsel[:, :, :],
                                     ALU.mult))
                link(V.tensor_reduce(weight_of[:, b, E:MAX_ITEMS], qt[:, :, :], AX.X, ALU.add))
            link(V.tensor_tensor(qt[:, :, :], e_idx[:, :, :].to_broadcast(over), qsel[:, :, :], ALU.mult))
            link(V.tensor_reduce(ids_f[:, E:MAX_ITEMS], qt[:, :, :], AX.X, ALU.add))
            link(V.tensor_copy(ids_f[:, 0:E], e_idx[:, 0, :]))
            V.tensor_copy(item_expert[:, :], ids_f[:, :]).then_inc(tables_ready, 1)

            def add_back(scattered_before, parts=range(8)):
                for j in parts:
                    b, c = j // 4, j % 4
                    dve.wait_ge(scattered, scattered_before + (j + 1))
                    cols = slice(c * BANK, (c + 1) * BANK)
                    V.tensor_tensor(acc[:, b, cols], acc[:, b, cols], bank[5 + j % 3][:, :], ALU.add)\
                     .then_inc(acc_added, 1)

            dve.wait_ge(tables_ready, 1)
            last_item = dve.value_load(last_index[0:1, 0:1], min_val=E - 1, max_val=MAX_ITEMS - 1)
            dve.wait_ge(acc_set, NB)

            def item(i, last=False):
                dve.wait_ge(gathered, i * 2 + 2)
                V.tensor_copy(x_row[:, :], bank[7][:, :]).then_inc(row_b_ready, 1)
                if not last:
                    for b in range(NB):
                        ins = V.tensor_scalar(pick[:, b, :], tok_of[:, 0:TOK], rank_of[:, b, bass.ds(i + 1, 1)],
                                              rinv[:, 4 + b:5 + b], ALU.is_equal, ALU.mult)
                    ins.then_inc(pick_ready, 1)
                for b in range(NB):
                    ins = V.tensor_scalar(place[:, b, :], tok_of[:, :], rank_of[:, b, bass.ds(i, 1)],
                                          weight_of[:, b, bass.ds(i, 1)], ALU.is_equal, ALU.mult)
                ins.then_inc(place_ready, 1)
                take_half(i, 1)
                add_back(i * 8)
                dve.wait_ge(sil_ready, i * 2 + 1)
                V.tensor_tensor(hid[TOK:P, :], sil[TOK:P, :], bank[0][TOK:P, :], ALU.mult)
                dve.wait_ge(sil_ready, i * 2 + 2)
                V.tensor_tensor(hid[0:TOK, :], sil[0:TOK, :], bank[1][0:TOK, :], ALU.mult).then_inc(hid_ready, 1)
                if last:
                    dve.wait_ge(step_done, i * STEPS + STEPS)
                    V.tensor_copy(y[:, 1, :], bank[3][:, :]).then_inc(last_y_ready, 1)
                else:
                    take_half(i + 1, 0)

            with dve.Fori(0, last_item) as i:
                item(i)
            item(last_item, last=True)

            def finish(b, c):
                cols = slice(c * PIECE, (c + 1) * PIECE)
                V.scalar_tensor_tensor(out=acc[:, b, cols], in0=acc[:, b, cols], scalar=rinv[:, b:b + 1],
                                       in1=final_gain[:, cols], op0=ALU.mult, op1=ALU.mult).then_inc(out_ready, 1)

            def take_root(b):
                dve.wait_ge(roots_done, 4 + b)
                V.reciprocal(rinv[:, b:b + 1], root[:, 4 + b:5 + b]).then_inc(rinv_ready, 1)
                dve.wait_ge(rinv_ready, 4 + b)

            add_back(last_item * 8 + 8, range(6))
            take_root(0)
            dve.wait_ge(gain_loaded, 32)
            finish(0, 0)
            add_back(last_item * 8 + 8, range(6, 8))
            finish(0, 1)
            take_root(1)
            finish(1, 0)
            finish(1, 1)

        @block.tensor
        def _(pe):
            T = nc.tensor
            pe.wait_ge(ident_ready, 1)

            def keep_warm(bank_no, products):
                for _ in range(products):
                    T.matmul(bank[bank_no][:, 0:P], ident[:, :], ident[:, :], start=True, stop=True)

            pe.wait_ge(vecs_loaded, 48)
            rows = 2 * KD + HEADS
            T.transpose(bank[0][:, 0:rows], vec_raw, ident[0:rows, 0:rows]).then_inc(vecs_transposed, 1)

            def transpose_pair(dst, src, g):
                for s in range(2):
                    for b in range(NB):
                        k = 2 * g + s
                        last = T.transpose(dst[:, s * SEQ + b * P:s * SEQ + (b + 1) * P],
                                           src[:, b, k * P:(k + 1) * P], ident[:, :])
                return last

            for g in range(2):
                pe.wait_ge((first_x_loaded, x_loaded[0])[g], 16)
                transpose_pair(bank[4 + g], x, g).then_inc(x_transposed, 1)

            def project_columns(bank_set, k, c, blocks=range(NB)):
                for b in blocks:
                    dst = bank[4 * bank_set + 2 * c + b][:, :]
                    hi, lo = (t[:, k, b * P:(b + 1) * P] for t in (act_hi, act_lo))
                    wh, wl = (t[:, k % 2, c * BANK:(c + 1) * BANK] for t in (w_hi, w_lo))
                    T.matmul(dst, hi, wh, start=(k == 0), stop=False)
                    T.matmul(dst, hi, wl, start=False, stop=False)
                    last = T.matmul(dst, lo, wh, start=False, stop=(k == KD - 1))
                return last

            def project_slab(bank_set, k):
                for c in range(2):
                    last = project_columns(bank_set, k, c)
                last.then_inc(tile_used, 1)

            pe.wait_ge(vecs_ready, 1)
            for k in range(KD):
                if 1 <= k < 7:
                    g = k + 1
                    if g % 2 == 0:
                        pe.wait_ge(x_loaded[g // 2], 16)
                    if g >= 4:
                        pe.wait_ge(x_scaled, g - 3)
                    transpose_pair(bank[4 + g % 4], x, g).then_inc(x_transposed, 1)
                if k == 12:
                    pe.wait_ge(ws_masked, 1)
                    for g in range(2):
                        pe.wait_ge(x_scaled, 5 + g)
                        for h in range(4):
                            last = T.transpose(bank[4 + g][:, h * P:(h + 1) * P], ws_raw[:, 4 * g + h, :],
                                               ident[:, :])
                        last.then_inc(ws_transposed, 1)
                if k % 2 == 0:
                    pe.wait_ge(act_ready, k // 2 + 1)
                pe.wait_ge(tile_split, k + 1)
                project_slab(0, k)
            pe.wait_ge(x_scaled, KD // 2)
            pe.wait_ge(ws_ready, 2)
            for k in range(KD):
                pe.wait_ge(tile_split, KD + k + 1)
                project_slab(1, k)
            pe.wait_ge(z_ready, 4)
            for k in range(KD):
                pe.wait_ge(tile_split, 2 * KD + k + 1)
                project_slab(0, k)

            def mix_heads(heads):
                for h in heads:
                    for b in range(NB):
                        last = T.matmul(bank[h % 4][:, b * HD:(b + 1) * HD], ws_t[:, h, :],
                                        v[:, b, h * HD:(h + 1) * HD], start=True, stop=True)
                    last.then_inc(mixed, 1)

            pe.wait_ge(z_ready, 8)
            for k in range(KD):
                if k == 8:
                    pe.wait_ge(v_ready, V_PARTS)
                    pe.wait_ge(z_ready, 12)
                    mix_heads(range(4))
                if k >= 12:
                    pe.wait_ge(gated, k - 11)
                    transpose_pair(bank[k - 12], u, k - 12).then_inc(gated_t, 1)
                pe.wait_ge(tile_split, 3 * KD + k + 1)
                project_slab(1, k)
            pe.wait_ge(act_ready, KD // 2 + 4)
            mix_heads(range(4, HEADS))

            pe.wait_ge(z_ready, 16)
            for k in range(KD):
                if 2 <= k < 6:
                    pe.wait_ge(gated, k + 3)
                    transpose_pair(bank[k - 2], u, k + 2).then_inc(gated_t, 1)
                if k >= 8 and k % 2 == 0:
                    pe.wait_ge(act_ready, KD // 2 + k // 2 + 1)
                pe.wait_ge(tile_split, 4 * KD + k + 1)
                project_slab(SET_OF[PIECES_IN], k)
            for k in range(KD - 2):
                pe.wait_ge(tile_split, 5 * KD + k + 1)
                project_slab(SET_OF[PIECES_IN + 1], k)
                if k == 7:
                    pe.wait_ge(h2_ready, 4)
                    for g in range(4):
                        transpose_pair(bank[4 + g], x, g).then_inc(h2_transposed, 1)
            final_set = SET_OF[PIECES_IN + 1]
            pe.wait_ge(tile_split, 6 * KD - 1)
            project_columns(final_set, KD - 2, 0)
            project_columns(final_set, KD - 2, 1, blocks=[0])
            pe.wait_ge(tile_split, 6 * KD)
            project_columns(final_set, KD - 1, 0).then_inc(half_done, 1)
            project_columns(final_set, KD - 2, 1, blocks=[1])
            project_columns(final_set, KD - 1, 1, blocks=[0]).then_inc(half_done, 1)
            project_columns(final_set, KD - 1, 1, blocks=[1]).then_inc(tile_used, 2)
            pe.wait_ge(h2_t_ready, 4)
            for g in range(4):
                if g % 2 == 0:
                    pe.wait_ge(h2_ready, 6 + g)
                transpose_pair(bank[4 + g], x, 4 + g).then_inc(h2_transposed, 1)

            pe.wait_ge(h2_ready, 8)
            pe.wait_ge(rwg_ready, 1)
            for k in range(KD):
                if k >= 8 and k % 2 == 0:
                    pe.wait_ge(h2_t_ready, k // 2 + 1)
                q = k % 4
                last = T.matmul(bank[0][q * QUAD:(q + 1) * QUAD, 0:SEQ], rwg[:, k, :], h2_t[:, k, :],
                                start=(k < 4), stop=(k >= KD - 4), tile_position=(0, q * QUAD))
            last.then_inc(quarters_done, 1)
            pe.wait_ge(quarter_ready, 1)
            pe.wait_ge(rwg_ready, 2)
            for b in range(NB):
                last = T.matmul(bank[1][:, b * E:(b + 1) * E], quarter[:, b * P:(b + 1) * P], fold[:, :],
                                start=True, stop=True)
            last.then_inc(logits_done, 1)
            keep_warm(4, 20)
            pe.wait_ge(assigned_ready, 1)
            flat = assigned[:, :, :].rearrange("p b e -> p (b e)")
            T.matmul(bank[2][:, 0:NB * E], before[:, :], flat, start=True, stop=False)
            T.matmul(bank[2][:, E:2 * E], ones[:, :], assigned[:, 0, :], start=False, stop=True)
            for b in range(NB):
                last = T.matmul(bank[3][:, 0:E], ones[:, :], assigned[:, b, :], start=(b == 0), stop=(b == NB - 1))
            last.then_inc(ranks_done, 1)

            def gather(jj):
                for b in range(NB):
                    for h in range(2):
                        c = 2 * jj + h
                        last = T.matmul(bank[6 + jj][h * TOK:(h + 1) * TOK, :], pick[:, b, :],
                                        x[:, b, c * BANK:(c + 1) * BANK], start=(b == 0), stop=(b == NB - 1))
                last.then_inc(gathered, 1)

            def transpose_rows(n, jj):
                pe.wait_ge((row_a_ready, row_b_ready)[jj], n + 1)
                for g in range(4):
                    last = T.transpose(bank[6 + jj][:, g * P:(g + 1) * P], x_row[:, g * P:(g + 1) * P], ident[:, :])
                last.then_inc(row_transposed, 1)

            def scatter(added_before, last=False):
                for j in range(8):
                    b, jj, h = j // 4, j % 4 // 2, j % 2
                    if last and j == 2:
                        pe.wait_ge(last_y_ready, 1)
                    if j >= 3:
                        pe.wait_ge(acc_added, added_before + (j - 2))
                    T.matmul(bank[5 + j % 3][:, :], back[h * TOK:(h + 1) * TOK, b * P:(b + 1) * P],
                             y[h * TOK:(h + 1) * TOK, jj, :], start=True, stop=True).then_inc(scattered, 1)

            keep_warm(4, 4)
            pe.wait_ge(pick_ready, 1)
            gather(0)
            keep_warm(4, 3)
            transpose_rows(0, 0)
            keep_warm(4, 5)
            pe.wait_ge(count_ready, 1)
            last_item = pe.value_load(last_index[0:1, 0:1], min_val=E - 1, max_val=MAX_ITEMS - 1)

            def item(i, last=False):
                for m in range(PIECE_UNITS):
                    if m == 0:
                        pe.wait_ge(xg_ready, i * 2 + 1)
                    for unit in (2 * m, 2 * m + 1):
                        pe.wait_ge(unit_loaded[slot_of(unit)], unit_count(i, unit))
                    for s in range(2):
                        for c in range(2):
                            for up in range(2):
                                at = TOK * ((up + c) % 2)
                                ins = T.matmul(bank[c][at:at + TOK, :], xg[:, 2 * m + s, :],
                                                slot(slot_of(2 * m + up))[:, s * F + c * BANK:s * F + (c + 1) * BANK],
                                                start=(m == 0 and s == 0), stop=(m == PIECE_UNITS - 1 and s == 1))
                    ins.then_inc(step_done, 1)
                    if m == 0:
                        gather(1)
                    if m == 1:
                        transpose_rows(i, 1)
                    if m == 3:
                        pe.wait_ge(y_ready, i + 1)
                        pe.wait_ge(back_ready, i + 1)
                        pe.wait_ge(xg_ready, i * 2 + 2)
                        scatter(i * 8)
                    if m == 5:
                        pe.wait_ge(acc_added, i * 8 + 8)
                        pe.wait_ge(place_ready, i + 1)
                        for b in range(NB):
                            ins = T.transpose(bank[5][:, b * P:(b + 1) * P], place[:, b, :], ident[:, :])
                        ins.then_inc(place_transposed, 1)
                        if not last:
                            pe.wait_ge(pick_ready, i + 2)
                            gather(0)
                pe.wait_ge(hid_ready, i + 1)
                for f in range(4):
                    ins = T.transpose(bank[4][:, f * P:(f + 1) * P], hid[:, f * P:(f + 1) * P], ident[:, :])
                ins.then_inc(hid_transposed, 1)
                if not last:
                    transpose_rows(i + 1, 0)
                pe.wait_ge(hid_t_ready, i + 1)
                for f in range(KF):
                    unit = 2 * PIECE_UNITS + f
                    pe.wait_ge(unit_loaded[slot_of(unit)], unit_count(i, unit))
                    hidden = hid_t[:, f % 4, TOK:P] if f < 4 else hid_t[:, f % 4, 0:TOK]
                    for c in range(4):
                        at = TOK * (c % 2)
                        ins = T.matmul(bank[2 + c // 2][at:at + TOK, :], hidden,
                                        slot(slot_of(unit))[:, c * BANK:(c + 1) * BANK],
                                        start=(f == 0), stop=(f == KF - 1))
                        if last and f == KF - 1 and c == 1:
                            ins.then_inc(last_y_half_done, 1)
                    ins.then_inc(step_done, 1)

            with pe.Fori(0, last_item) as i:
                item(i)
            item(last_item, last=True)
            pe.wait_ge(y_ready, last_item + 2)
            pe.wait_ge(back_ready, last_item + 2)
            scatter(last_item * 8 + 8, last=True)


_INS = ['x', 'norm_mix_g', 'norm_ffn_g', 'final_g', 'a_w_in', 'a_v_gain', 'a_w_s', 'a_b_s', 'a_w_out',
        'router_w', 'router_b', 'moe_w_gate', 'moe_w_up', 'moe_w_down']


def kernel(**inputs):
    import numpy as np
    import concourse.bacc as bacc
    from concourse.bass_utils import run_bass_kernel_spmd

    nc = bacc.Bacc("TRN2", target_bir_lowering=False, num_devices=1)
    arrays, args = {}, []
    for name in _INS:
        a = np.ascontiguousarray(inputs[name])
        arrays[f"in_{name}"] = a
        args.append(nc.dram_tensor(f"in_{name}", a.shape, mybir.dt.from_np(a.dtype), kind="ExternalInput").ap())
    shape = inputs['x'].shape
    args.append(nc.dram_tensor("out", shape, mybir.dt.float32, kind="ExternalOutput").ap())
    hybrid_trunk_kernel(nc, *args)
    r = run_bass_kernel_spmd(nc, [arrays], core_ids=[0])
    return r.results[0]["out"]
```
